# Optimizing a Trainium2 kernel written in Bass

```python
import jax, jax.numpy as jnp
from jax import lax
import numpy as np

D_MODEL = 2048
BATCH = 1
SEQ = 512
DEPTH = 1

MIX_WIDTH = D_MODEL
HEAD_DIM = 128
ATTN_WIDTH = MIX_WIDTH // 2
ATTN_HEADS = ATTN_WIDTH // HEAD_DIM
GMLP_GROUP_DIM = 128
GMLP_WIDTH = MIX_WIDTH - ATTN_WIDTH
GMLP_GROUPS = GMLP_WIDTH // GMLP_GROUP_DIM
CHUNK = 128
Q_BLOCK = 128
D_FF = 4 * D_MODEL
N_MOD = 6
IN_COLS = 3 * ATTN_WIDTH + ATTN_HEADS + 2 * GMLP_WIDTH
EPS = 1e-6

kernel_name = "hybrid_fox_gmlp_adaln_block"

def rms_norm(x, g):
    xf = x.astype(jnp.float32)
    y = xf * lax.rsqrt(jnp.mean(xf * xf, axis=-1, keepdims=True) + EPS)
    return (y * g.astype(jnp.float32)).astype(x.dtype)

def layer_norm_nobias(x, g):
    xf = x.astype(jnp.float32)
    mu = jnp.mean(xf, axis=-1, keepdims=True)
    xc = xf - mu
    y = xc * lax.rsqrt(jnp.mean(xc * xc, axis=-1, keepdims=True) + EPS)
    return y * g.astype(jnp.float32)

def modulate(h, shift, scale):
    return h * (1.0 + scale[:, None, :]) + shift[:, None, :]

def forgetting_attention(q, k, v, f_logit):
    B, S, H, Dh = q.shape
    nblk = S // Q_BLOCK
    scale = 1.0 / np.sqrt(Dh).astype(np.float32)
    F = jnp.cumsum(jax.nn.log_sigmoid(f_logit.astype(jnp.float32)), axis=1)
    F_bhs = F.transpose(0, 2, 1)
    kf = k.astype(jnp.float32)
    vf = v.astype(jnp.float32)
    qb = q.astype(jnp.float32).reshape(B, nblk, Q_BLOCK, H, Dh).transpose(1, 0, 3, 2, 4)
    Fq = F_bhs.reshape(B, H, nblk, Q_BLOCK).transpose(2, 0, 1, 3)
    kpos = jnp.arange(S)

    def block(args):
        i, q_blk, F_blk = args
        s = jnp.einsum('bhqd,bshd->bhqs', q_blk, kf) * scale
        s = s + F_blk[..., None] - F_bhs[:, :, None, :]
        qpos = i * Q_BLOCK + jnp.arange(Q_BLOCK)
        causal = kpos[None, :] <= qpos[:, None]
        s = jnp.where(causal[None, None], s, -jnp.inf)
        p = jax.nn.softmax(s, axis=-1)
        return jnp.einsum('bhqs,bshd->bqhd', p, vf)

    out = lax.map(block, (jnp.arange(nblk), qb, Fq))
    return out.transpose(1, 0, 2, 3, 4).reshape(B, S, H * Dh)

def chunked_spatial_gating(u, v, g_ln, w_s, b_s):
    B, S, G, C = v.shape
    n = S // CHUNK
    vn = layer_norm_nobias(v, g_ln)
    vc = vn.reshape(B, n, CHUNK, G, C)
    mask = jnp.tril(jnp.ones((CHUNK, CHUNK), dtype=jnp.float32))
    w = w_s.astype(jnp.float32) * mask[None]
    z = jnp.einsum('gts,bnsgc->bntgc', w, vc) + b_s.astype(jnp.float32).T[None, None, :, :, None]
    out = u.astype(jnp.float32) * z.reshape(B, S, G, C)
    return out.reshape(B, S, G * C)

def setup_inputs(seed: int = 0) -> dict:
    key = jax.random.key(seed)
    ks = jax.random.split(key, 20)
    f32 = jnp.float32
    nrm = lambda k, shp, s: jax.random.normal(k, shp, f32) * s
    gain = lambda k, shp: 1.0 + 0.02 * jax.random.normal(k, shp, f32)
    x = jax.random.normal(ks[0], (BATCH, SEQ, D_MODEL), f32)
    c = jax.random.normal(ks[1], (BATCH, D_MODEL), f32)
    w_ada = nrm(ks[2], (DEPTH, D_MODEL, N_MOD * D_MODEL), 0.5 * D_MODEL ** -0.5)
    b_ada = nrm(ks[3], (DEPTH, N_MOD * D_MODEL), 0.02)
    g_mix = gain(ks[4], (DEPTH, D_MODEL))
    w_in = nrm(ks[5], (DEPTH, D_MODEL, IN_COLS), D_MODEL ** -0.5)
    b_f = jax.random.uniform(ks[6], (DEPTH, ATTN_HEADS), f32, 1.0, 4.0)
    g_q = gain(ks[7], (DEPTH, HEAD_DIM))
    g_k = gain(ks[8], (DEPTH, HEAD_DIM))
    g_sgu = gain(ks[9], (DEPTH, GMLP_GROUPS, GMLP_GROUP_DIM))
    w_s = nrm(ks[10], (DEPTH, GMLP_GROUPS, CHUNK, CHUNK), 0.5 * CHUNK ** -0.5)
    b_s = 1.0 + nrm(ks[11], (DEPTH, GMLP_GROUPS, CHUNK), 0.1)
    w_out = nrm(ks[12], (DEPTH, MIX_WIDTH, D_MODEL), MIX_WIDTH ** -0.5)
    g_ffn = gain(ks[13], (DEPTH, D_MODEL))
    w_ff1 = nrm(ks[14], (DEPTH, D_MODEL, D_FF), D_MODEL ** -0.5)
    w_ff2 = nrm(ks[15], (DEPTH, D_FF, D_MODEL), D_FF ** -0.5)
    return {"x": x, "c": c, "w_ada": w_ada, "b_ada": b_ada, "g_mix": g_mix, "w_in": w_in,
            "b_f": b_f, "g_q": g_q, "g_k": g_k, "g_sgu": g_sgu, "w_s": w_s, "b_s": b_s,
            "w_out": w_out, "g_ffn": g_ffn, "w_ff1": w_ff1, "w_ff2": w_ff2}

def reference(x, c, w_ada, b_ada, g_mix, w_in, b_f, g_q, g_k, g_sgu, w_s, b_s,
              w_out, g_ffn, w_ff1, w_ff2):
    B, S, D = x.shape
    H, Dh, G, C = ATTN_HEADS, HEAD_DIM, GMLP_GROUPS, GMLP_GROUP_DIM
    c_act = jax.nn.silu(c)
    for l in range(DEPTH):
        mod = c_act @ w_ada[l] + b_ada[l]
        shift1, scale1, gate1, shift2, scale2, gate2 = jnp.split(mod, N_MOD, axis=-1)

        h = modulate(rms_norm(x, g_mix[l]), shift1, scale1)
        proj = h @ w_in[l]
        o = 0
        q = proj[..., o:o + ATTN_WIDTH]; o += ATTN_WIDTH
        k = proj[..., o:o + ATTN_WIDTH]; o += ATTN_WIDTH
        v = proj[..., o:o + ATTN_WIDTH]; o += ATTN_WIDTH
        f_logit = proj[..., o:o + H]; o += H
        u_g = proj[..., o:o + GMLP_WIDTH]; o += GMLP_WIDTH
        v_g = proj[..., o:o + GMLP_WIDTH]

        q = rms_norm(q.reshape(B, S, H, Dh), g_q[l])
        k = rms_norm(k.reshape(B, S, H, Dh), g_k[l])
        v = v.reshape(B, S, H, Dh)
        attn = forgetting_attention(q, k, v, f_logit + b_f[l]).astype(x.dtype)

        u_g = jax.nn.gelu(u_g).reshape(B, S, G, C)
        v_g = jax.nn.gelu(v_g).reshape(B, S, G, C)
        sgu = chunked_spatial_gating(u_g, v_g, g_sgu[l], w_s[l], b_s[l]).astype(x.dtype)

        mix = jnp.concatenate([attn, sgu], axis=-1) @ w_out[l]
        x = x + gate1[:, None, :] * mix

        h2 = modulate(rms_norm(x, g_ffn[l]), shift2, scale2)
        ff = jnp.square(jax.nn.relu(h2 @ w_ff1[l])) @ w_ff2[l]
        x = x + gate2[:, None, :] * ff
    return x


_drawn_inputs = setup_inputs


def setup_inputs(seed=0):
    import zlib

    import numpy as np

    out = dict(_drawn_inputs(seed))
    spreads = {}
    factors = {'g_mix': 8.0, 'g_q': 8.0, 'g_k': 8.0, 'g_sgu': 8.0, 'b_s': 3.582, 'g_ffn': 6.105}
    for name, (base, spread) in spreads.items():
        noise = np.random.default_rng([zlib.crc32(name.encode()), seed]).standard_normal(out[name].shape)
        drawn = base * np.exp(spread * noise) if base else spread * noise
        out[name] = __import__('jax').numpy.asarray(drawn.astype(out[name].dtype))
    for name, factor in factors.items():
        out[name] = (out[name] * factor).astype(out[name].dtype)
    return out
```

```python
from contextlib import ExitStack

import concourse.bass as bass
from concourse import mybir

P = 128
F32 = mybir.dt.float32
F32R = mybir.dt.float32r
BF16 = mybir.dt.bfloat16
ALU = mybir.AluOpType
ACT = mybir.ActivationFunctionType
AX_X = mybir.AxisListType.X
EPS = 1e-6
NEG = -1.0e30


def block_program(nc, x, c, w_ada, b_ada, g_mix, w_in, b_f, g_q, g_k, g_sgu, w_s, b_s,
                  w_out, g_ffn, w_ff1, w_ff2, out):
    _, S, D = x.shape
    H = b_f.shape[1]
    G = g_sgu.shape[1]
    DH = g_q.shape[1]
    AW = H * DH
    GW = G * P
    DFF = w_ff1.shape[2]
    KC = D // P
    ST = S // P
    HP = H // 2
    FC = DFF // D
    PAIR = 2 * P
    SLOTS = KC // 2
    NPAIR = D // PAIR
    BODIES = NPAIR // 2
    LEAD = 2
    STEP_PAIRS = 5
    STEP_SLOTS = STEP_PAIRS * SLOTS
    OUT_PAIR = HP * STEP_PAIRS
    FF_PAIR = OUT_PAIR + NPAIR
    RAW = 4
    SPLIT = 4
    assert (S, KC, ST, DH, H, G, AW, GW) == (512, 16, 4, P, G, H, GW, AW) and FC == 4

    COL_K, COL_V, COL_F = AW, 2 * AW, 3 * AW
    COL_U = COL_F + H
    COL_VG = COL_U + GW
    SHIFT1, SCALE1, GATE1, SHIFT2, SCALE2, GATE2 = (n * KC for n in range(6))

    GRP = 4
    GRPS = KC // GRP
    GC = GRP * P
    MRING = 8
    MB = (GATE2 - GATE1) * P // HP // 2
    MBT = MB // P
    MOD_A = [2, 3, 4, 5, 6, 7, 8, 9, 9, 11, 13, 14, 15, 16, 17, 17]
    MOD_B = [21, 22, 23, 24, 25, 26, 27, 28, 29, 30, 32, 34, 35, 36, 37, 37]
    MO = D // BODIES
    MOT = MO // P
    MOD_O = [2, 3, 4, 5, 6, 7, 8, 8, 9, 9, 10, 11, 12, 12, 13, 13]
    SCORE_AT = [20, 21, 22, 23, 26, 27, 28, 29]
    assert len(MOD_A) == len(MOD_B) == len(MOD_O) == KC

    with ExitStack() as ctx:
        def sb(name, shape, dt=F32, where=ctx):
            return where.enter_context(nc.sbuf_tensor(name, shape, dt))

        def sem(name):
            return ctx.enter_context(nc.semaphore(name))

        bank_a = ctx.enter_context(nc.psum_tensor("bank_a", [P, 2, S], F32))
        bank_b = ctx.enter_context(nc.psum_tensor("bank_b", [P, 2, S], F32))
        bank_s = ctx.enter_context(nc.psum_tensor("bank_s", [P, 2, S], F32))
        bank_t = ctx.enter_context(nc.psum_tensor("bank_t", [P, S], F32))
        bank_o = ctx.enter_context(nc.psum_tensor("bank_o", [P, S], F32))

        ident = sb("ident", [P, P])
        ident_bf = sb("ident_bf", [P, P], BF16)
        mask_bf = sb("mask_bf", [P, P], BF16)
        mask01 = sb("mask01", [P, P])
        ones = sb("ones", [P, P])
        cols = sb("cols", [P, 2])
        rows_a = sb("rows_a", [P, P])
        rows_b = sb("rows_b", [P, P])
        vec_a = sb("vec_a", [P, P])
        vec_b = sb("vec_b", [P, P])
        c_act = sb("c_act", [P, KC])
        gq_scaled = sb("gq_scaled", [P, 1])
        bf_col = sb("bf_col", [H, 1])
        mod = sb("mod", [P, 6 * KC])
        a1 = sb("a1", [P, KC])
        a2 = sb("a2", [P, KC])
        x_sum = sb("x_sum", [P, ST])
        x_root = sb("x_root", [P, ST])
        x_inv = sb("x_inv", [P, ST])
        neg_sel = sb("neg_sel", [P, H])
        sel_cur = sb("sel_cur", [P, 2, P], F32R)
        f_split = sb("f_split", [P, S], F32R)
        wf_raw = sb("wf_raw", [P, KC, H])
        wf = sb("wf", [P, KC, 2 * H], F32R)
        f_two = sb("f_two", [P, ST, 2 * H])
        f_nat = sb("f_nat", [P, ST, H])
        neg_max = sb("neg_max", [P, 8])
        row_sum = sb("row_sum", [P, 8])
        row_inv = sb("row_inv", [P, 8])
        vg_stats = sb("vg_stats", [P, 2, ST, 6])
        vg_mv = sb("vg_mv", [P, 2, ST, 2])
        vg_root = sb("vg_root", [P, 2, ST])
        vg_inv = sb("vg_inv", [P, 2, ST])
        raw = sb("raw", [P, RAW, 4, PAIR])
        w_hi = sb("w_hi", [P, SPLIT, 2, PAIR], F32R)
        w_lo = sb("w_lo", [P, SPLIT, 2, PAIR], F32R)
        h_hi = sb("h_hi", [P, KC, S], F32R)
        early = ExitStack()
        xhat = sb("xhat", [P, KC, S], F32, early)
        early.close()
        h_lo = sb("h_lo", [P, KC, S], F32R)
        early = ExitStack()
        mod_tile = sb("mod_tile", [P, MRING, 2, GC], F32, early)
        mod_acc = sb("mod_acc", [P, 2, 2, GC], F32, early)
        early.close()
        mix_hi = sb("mix_hi", [P, KC, S], F32R)
        mix_lo = sb("mix_lo", [P, KC, S], F32R)
        tmp = sb("tmp", [P, 2, S])
        part = sb("part", [P, 2, S])
        early = ExitStack()
        x_nat = sb("x_nat", [P, ST, D], F32, early)
        early.close()
        early = ExitStack()
        q_t = sb("q_t", [P, 2, S], F32, early)
        k_t = sb("k_t", [P, 2, S], F32, early)
        v_n = sb("v_n", [P, 2, ST, P], F32, early)
        vg_n = sb("vg_n", [P, 2, ST, P], F32, early)
        prob = sb("prob", [P, ST, S], F32, early)
        prob_t = sb("prob_t", [P, ST, S], F32, early)
        early.close()
        x1 = sb("x1", [P, KC, S])
        early = ExitStack()
        ws_nat = sb("ws_nat", [P, 2, P], F32, early)
        ws_t = sb("ws_t", [P, 2, P], F32, early)
        bs_all = sb("bs_all", [P, 2, P], F32, early)
        mtile = sb("mtile", [P, 2, MB], F32, early)
        macc = sb("macc", [P, MB], F32, early)
        early.close()
        x_stage = sb("x_stage", [P, ST, PAIR])
        otile = sb("otile", [P, 2, MO])
        oacc = sb("oacc", [P, MO])
        inv, sq_acc = part[:, 0, :], part[:, 1, :]
        f_x, f_y = tmp[0:H, 0, :], tmp[0:H, 1, :]
        f_cum, f_ones = part[0:H, 0, :], part[0:H, 1, :]

        consts_made = sem("consts_made")
        rows_in = sem("rows_in")
        small_in = sem("small_in")
        rows_turned = sem("rows_turned")
        vecs_ready = sem("vecs_ready")
        c_ready = sem("c_ready")
        gq_ready = sem("gq_ready")
        x_in = [sem(f"x_in{i}") for i in range(ST)]
        x_squared = sem("x_squared")
        x_rooted = sem("x_rooted")
        x_inverted = sem("x_inverted")
        x_normed = sem("x_normed")
        x_turned = sem("x_turned")
        xhat_ready = sem("xhat_ready")
        mod_in = [sem(f"mod_in{i}") for i in range(MRING)]
        mod_step = sem("mod_step")
        mod_sums = sem("mod_sums")
        mod_added = sem("mod_added")
        a1_ready = sem("a1_ready")
        h_full = sem("h_full")
        h_hi_ready = sem("h_hi_ready")
        h_ready = sem("h_ready")
        wf_rounded = sem("wf_rounded")
        wf_ready = sem("wf_ready")
        f_sums = sem("f_sums")
        f_biased = sem("f_biased")
        f_act = sem("f_act")
        f_log = sem("f_log")
        f_summed = sem("f_summed")
        f_hi_ready = sem("f_hi_ready")
        f_ready = sem("f_ready")
        f_cleared = sem("f_cleared")
        raw_in = [sem(f"raw_in{i}") for i in range(RAW)]
        w_rounded = sem("w_rounded")
        w_split = sem("w_split")
        slot_used = sem("slot_used")
        ws_in = sem("ws_in")
        bs_in = sem("bs_in")
        ws_turned = sem("ws_turned")
        ws_ready = sem("ws_ready")
        sel_ready = sem("sel_ready")
        squares = sem("squares")
        norm_sums = sem("norm_sums")
        norm_root = sem("norm_root")
        norm_inv = sem("norm_inv")
        qk_ready = sem("qk_ready")
        scores = sem("scores")
        maxima = sem("maxima")
        exps = sem("exps")
        sums_inv = sem("sums_inv")
        probs = sem("probs")
        probs_turned = sem("probs_turned")
        probs_t = sem("probs_t")
        v_part = sem("v_part")
        v_turned = sem("v_turned")
        v_ready = sem("v_ready")
        attn_sums = sem("attn_sums")
        attn_hi = sem("attn_hi")
        attn_ready = sem("attn_ready")
        vg_part = sem("vg_part")
        vg_turned = sem("vg_turned")
        vg_stat = sem("vg_stat")
        vg_agg = sem("vg_agg")
        vg_rooted = sem("vg_rooted")
        vg_inverted = sem("vg_inverted")
        vg_ready = sem("vg_ready")
        z_sums = sem("z_sums")
        z_ready = sem("z_ready")
        gate_ready = sem("gate_ready")
        gated = sem("gated")
        sgu_hi = sem("sgu_hi")
        sgu_ready = sem("sgu_ready")
        mtile_in = [sem(f"mtile_in{i}") for i in range(2)]
        m_step = sem("m_step")
        m_sums = sem("m_sums")
        m_added = sem("m_added")
        otile_in = [sem(f"otile_in{i}") for i in range(2)]
        o_step = sem("o_step")
        o_sums = sem("o_sums")
        o_added = sem("o_added")
        stage_in = sem("stage_in")
        stage_turned = sem("stage_turned")
        x1_old = sem("x1_old")
        x1_ready = [sem(f"x1_ready{q}") for q in range(2)]
        x1_square = sem("x1_square")
        sq_added = sem("sq_added")
        sq_sums = sem("sq_sums")
        f_turned = sem("f_turned")
        f_copied = sem("f_copied")
        f_joined = sem("f_joined")
        sq_root = sem("sq_root")
        sq_cleared = sem("sq_cleared")
        inv_ready = sem("inv_ready")
        a2_ready = sem("a2_ready")
        h2_scaled = sem("h2_scaled")
        h2_hi = sem("h2_hi")
        h2_ready = sem("h2_ready")
        relu_ready = [sem(f"relu_ready{q}") for q in range(2)]
        ff_square = sem("ff_square")
        ff_hi = sem("ff_hi")
        ff_ready = sem("ff_ready")
        ff_added = [sem(f"ff_added{q}") for q in range(2)]
        y_turned = sem("y_turned")
        y_ready = sem("y_ready")
        y_out = sem("y_out")

        w_in_v = w_in[0].rearrange("(k p) n -> p k n", p=P)
        w_out_v = w_out[0].rearrange("(g h c p) n -> p h g c n", g=2, h=HP, p=P)
        w_ff1_v = w_ff1[0].rearrange("(k p) n -> p k n", p=P)
        w_ff2_v = w_ff2[0].rearrange("(c k p) n -> p c k n", c=FC, p=P)
        ada_v = w_ada[0].rearrange("(k p) (m n) -> k p m n", p=P, m=6)
        ada_flat = w_ada[0].rearrange("(k p) n -> k p n", p=P)
        x_v = x[0].rearrange("(i p) d -> p i d", p=P)
        out_v = out[0].rearrange("(i p) d -> p i d", p=P)
        b_s_v = b_s[0].rearrange("g t -> (g t)")

        block = ctx.enter_context(nc.Block())

        @block.sync
        def _(sp):
            sp.wait_ge(consts_made, 6)
            sp.dma_start(rows_b[0:KC, :], c.rearrange("a (k p) -> (a k) p", p=P)).then_inc(rows_in, 16)
            sp.dma_start(rows_a[0:6 * KC, :], b_ada.rearrange("a (k p) -> (a k) p", p=P)).then_inc(rows_in, 16)
            sp.dma_start(rows_a[6 * KC:7 * KC, :], g_mix.rearrange("a (k p) -> (a k) p", p=P)).then_inc(rows_in, 16)
            sp.dma_start(rows_a[7 * KC:8 * KC, :], g_ffn.rearrange("a (k p) -> (a k) p", p=P)).then_inc(rows_in, 16)
            sp.dma_start(rows_b[KC:KC + G, :], g_sgu[0]).then_inc(rows_in, 16)
            sp.dma_start(rows_b[KC + G:KC + G + 1, :], g_q).then_inc(rows_in, 16)
            sp.dma_start(rows_b[KC + G + 1:KC + G + 2, :], g_k).then_inc(rows_in, 16)
            for i in range(ST):
                sp.dma_start(x_nat[:, i, :], x_v[:, i, :]).then_inc(x_in[i], 16)

            def mod_load(g, k):
                sp.dma_start(mod_tile[:, k % MRING, :, :],
                             ada_v[k, :, 0:2, bass.ds(g * GC, GC)]).then_inc(mod_in[k % MRING], 16)

            for k in range(MRING):
                mod_load(0, k)
            for k in range(MRING, KC):
                sp.wait_ge(mod_step, k - MRING + 1)
                mod_load(0, k)
            with sp.Fori(1, GRPS) as g:
                for k in range(KC):
                    sp.wait_ge(mod_step, g * KC + (k - MRING + 1))
                    mod_load(g, k)
            sp.dma_start(bf_col[:, :], b_f.rearrange("a h -> h a")).then_inc(small_in, 16)
            sp.dma_start(wf_raw[:, :, :], w_in_v[:, :, COL_F:COL_F + H]).then_inc(small_in, 16)

            def tile_slot(steps, at):
                return steps[at - 2] + LEAD if at >= 2 else 0

            def chunk_load(pair, n, src):
                sp.wait_ge(w_split, pair * SLOTS + 2 * n + 2)
                sp.dma_start(raw[:, n, :, :], src).then_inc(raw_in[n], 32)

            with sp.Fori(0, HP) as hp:
                for j in range(STEP_SLOTS):
                    if j % 2 == 0:
                        col = (0, COL_K, COL_V, COL_VG, COL_U)[j // SLOTS]
                        n = (j % SLOTS) // 2
                        chunk_load(hp * STEP_PAIRS + j // SLOTS, n,
                                   w_in_v[:, 4 * n:4 * n + 4, bass.ds(hp * PAIR + col, PAIR)])
                    if j == 1:
                        sp.wait_ge(ws_turned, hp)
                        sp.dma_start(ws_nat[:, :, :], w_s[0].rearrange("g t s -> t g s")[:, bass.ds(hp * 2, 2), :]).then_inc(ws_in, 16)
                    if j == 4:
                        sp.wait_ge(z_ready, hp * 2)
                        sp.dma_start(bs_all[:, :, :].rearrange("p g t -> p (g t)"),
                                     b_s_v[bass.ds(hp * PAIR, PAIR)].partition_broadcast(P)).then_inc(bs_in, 16)
                    for at in range(2 * KC):
                        if tile_slot(MOD_A + MOD_B, at) != j:
                            continue
                        k, blk = at % KC, at // KC
                        sp.wait_ge(m_step, hp * (2 * KC) + max(at - 1, 0))
                        sp.dma_start(mtile[:, at % 2, :],
                                     ada_flat[k, :, bass.ds(hp * (2 * MB) + (GATE1 * P + blk * MB), MB)]
                                     ).then_inc(mtile_in[at % 2], 16)
            with sp.Fori(0, BODIES) as b:
                for q in range(2):
                    for n in range(4):
                        sp.wait_ge(w_split, (b * 2 + (OUT_PAIR + q)) * SLOTS + 2 * n + 2)
                        for g in range(2):
                            sp.dma_start(raw[:, n, 2 * g:2 * g + 2, :],
                                         w_out_v[:, n, g, :, bass.ds(b * (2 * PAIR) + q * PAIR, PAIR)]).then_inc(raw_in[n], 16)
                        if n == 0:
                            sp.wait_ge(stage_turned, b * 4 + 2 * q)
                            sp.wait_ge(m_step, HP * 2 * KC)
                            sp.wait_ge(m_sums, 2 * HP)
                            sp.wait_ge(z_ready, 2 * HP)
                            sp.dma_start(x_stage[:, :, :],
                                         x_v[:, :, bass.ds(b * (2 * PAIR) + q * PAIR, PAIR)]).then_inc(stage_in, 16)
                        for at in range(KC):
                            if tile_slot(MOD_O, at) // 2 != q * 4 + n:
                                continue
                            sp.wait_ge(o_step, b * KC + max(at - 1, 0))
                            sp.dma_start(otile[:, at % 2, :],
                                         ada_flat[at, :, bass.ds(b * MO + GATE2 * P, MO)]
                                         ).then_inc(otile_in[at % 2], 16)

            def ff1_loads(ch, b):
                for q in range(2):
                    for n in range(4):
                        chunk_load(ch * (2 * NPAIR) + (b * 2 + (FF_PAIR + q)), n,
                                   w_ff1_v[:, 4 * n:4 * n + 4, bass.ds(ch * D + (b * (2 * PAIR) + q * PAIR), PAIR)])

            def ff2_loads(ch, b):
                for q in range(2):
                    for n in range(4):
                        chunk_load(ch * (2 * NPAIR) + (b * 2 + (FF_PAIR + NPAIR + q)), n,
                                   w_ff2_v[:, ch, 4 * n:4 * n + 4, bass.ds(b * (2 * PAIR) + q * PAIR, PAIR)])

            with sp.Fori(0, FC) as ch:
                with sp.Fori(0, BODIES) as b:
                    ff1_loads(ch, b)
                with sp.Fori(0, BODIES) as b:
                    ff2_loads(ch, b)
            sp.wait_ge(y_out, 16 * NPAIR)

        @block.gpsimd
        def _(pool):
            pool.memset(ones[:, :], 1.0).then_inc(consts_made, 1)
            pool.memset(cols[:, 0:1], EPS).then_inc(consts_made, 1)
            pool.memset(cols[:, 1:2], 1.0).then_inc(consts_made, 1)
            pool.memset(mask_bf[:, :], 0.0).then_inc(consts_made, 1)
            pool.memset(neg_sel[:, :], 0.0).then_inc(consts_made, 1)
            pool.memset(rows_b[:, :], 0.0).then_inc(consts_made, 1)
            pool.wait_ge(consts_made, 6)
            pool.affine_select(out=ident[:, :], in_=ones[:, :], compare_op=ALU.is_equal, fill=0.0, base=0,
                               pattern=[[-1, P]], channel_multiplier=1).then_inc(consts_made, 1)
            pool.affine_select(out=mask01[:, :], in_=ones[:, :], compare_op=ALU.is_ge, fill=0.0, base=0,
                               pattern=[[1, P]], channel_multiplier=-1).then_inc(consts_made, 1)
            pool.affine_select(out=mask_bf[:, :], in_=mask_bf[:, :], compare_op=ALU.is_ge, fill=NEG, base=0,
                               pattern=[[-1, P]], channel_multiplier=1).then_inc(consts_made, 1)
            pool.wait_ge(consts_made, 9)
            pool.tensor_copy(ident_bf[:, :], ident[:, :]).then_inc(consts_made, 1)
            for at in (0, 32):
                pool.affine_select(out=neg_sel[:, :], in_=neg_sel[:, :], compare_op=ALU.not_equal, fill=-1.0,
                                   base=-at, pattern=[[-1, H]], channel_multiplier=1).then_inc(consts_made, 1)
                pool.wait_ge(consts_made, 11 + (at > 0))

        CONSTS = 12

        @block.scalar
        def _(act):
            def round_slot(pair0, j):
                n = (j % SLOTS) // 2
                act.wait_ge(raw_in[n], pair0 * 32 + 32 * (j // SLOTS + 1))
                act.wait_ge(slot_used, pair0 * SLOTS + (j + 1))
                act.activation(w_hi[:, j % SPLIT, :, :], raw[:, n, 2 * (j % 2):2 * (j % 2) + 2, :],
                               ACT.Copy).then_inc(w_rounded, 1)

            act.wait_ge(consts_made, CONSTS)
            act.wait_ge(vecs_ready, 2)
            act.activation(c_act[:, :], vec_b[:, 0:KC], ACT.Silu).then_inc(c_ready, 1)
            for i in range(ST):
                act.wait_ge(x_in[i], 16)
                act.activation(xhat[:, 4 * i:4 * i + 4, :], x_nat[:, i, :].rearrange("p (k n) -> p k n", k=4),
                               ACT.Square, accum_out=x_sum[:, i:i + 1]).then_inc(x_squared, 1)
            act.wait_ge(x_squared, ST)
            act.activation(x_root[:, :], x_sum[:, :], ACT.Sqrt, bias=cols[:, 0:1], scale=1.0 / D).then_inc(x_rooted, 1)
            act.wait_ge(x_inverted, 1)
            for i in range(ST):
                act.activation(x_nat[:, i, :], x_nat[:, i, :], ACT.Copy, scale=x_inv[:, i:i + 1]).then_inc(x_normed, 1)
            with act.Fori(0, KC // 2) as t:
                for a in range(2):
                    act.wait_ge(consts_made, CONSTS)
                    act.wait_ge(x_turned, t * 2 + (a + 1))
                    act.activation(xhat[:, bass.ds(t * 2 + a, 1), :], bank_s[:, a:a + 1, :], ACT.Copy).then_inc(xhat_ready, 1)
            with act.Fori(0, GRPS) as g:
                act.wait_ge(a1_ready, g + 1)
                for t in range(GRP):
                    act.wait_ge(consts_made, CONSTS)
                    act.activation(h_hi[:, bass.ds(g * GRP + t, 1), :], xhat[:, bass.ds(g * GRP + t, 1), :], ACT.Identity,
                                   scale=a1[:, bass.ds(g * GRP + t, 1)],
                                   bias=mod[:, bass.ds(g * GRP + t, 1)]).then_inc(h_hi_ready, 1)
            act.wait_ge(small_in, 32)
            act.activation(wf[:, :, 0:H], wf_raw[:, :, :], ACT.Copy).then_inc(wf_rounded, 1)
            for j in range(LEAD):
                round_slot(0, j)
            act.wait_ge(f_sums, 1)
            act.activation(f_two[:, :, :], bank_o[:, 0:ST * 2 * H].rearrange("p (i h) -> p i h", i=ST), ACT.Copy).then_inc(f_copied, 1)
            act.wait_ge(f_biased, 1)
            act.activation(f_y, f_x, ACT.Abs).then_inc(f_act, 1)
            act.wait_ge(f_act, 1)
            act.activation(f_y, f_y, ACT.Exp, scale=-1.0).then_inc(f_act, 1)
            act.wait_ge(f_act, 2)
            act.activation(f_y, f_y, ACT.Ln, bias=cols[0:H, 1:2]).then_inc(f_act, 1)

            def squares_of(hp, e, bank):
                act.activation(tmp[:, e % 2, :], bank[:, e % 2, :], ACT.Square).then_inc(squares, 1)

            def roots_of(hp, e):
                act.wait_ge(norm_sums, hp * 4 + (e + 1))
                src = (bank_s[:, 0, :], bank_s[:, 1, :], bank_t[:, :], bank_o[:, :])[e]
                act.activation(tmp[:, e % 2, :], src, ACT.Sqrt, bias=cols[:, 0:1], scale=1.0 / DH).then_inc(norm_root, 1)

            def exp_of(hp, t):
                n = P * (t % ST + 1)
                act.wait_ge(maxima, hp * 8 + (t + 1))
                act.wait_ge(probs_turned, hp * 8 + max(t - ST + 1, 0))
                act.activation(prob[:, t % ST, 0:n], bank_s[:, t % 2, 0:n], ACT.Exp, bias=neg_max[:, t:t + 1],
                               accum_out=row_sum[:, t:t + 1]).then_inc(exps, 1)

            def copy_prob_t(hp, t):
                i = t % ST
                act.wait_ge(probs_turned, hp * 8 + (t + 1))
                if t >= ST:
                    act.wait_ge(attn_sums, hp * 2 + 1)
                act.activation(prob_t[:, 0:i + 1, P * i:P * (i + 1)],
                               bank_t[:, 0:P * (i + 1)].rearrange("p (j q) -> p j q", q=P), ACT.Copy).then_inc(probs_t, 1)

            def slot_done(pair0, j):
                act.wait_ge(slot_used, pair0 * SLOTS + (j + 1 + SPLIT))

            with act.Fori(0, HP) as hp:
                pair0 = hp * STEP_PAIRS
                for j in range(STEP_SLOTS):
                    round_slot(pair0, j + LEAD)
                    if j == 7:
                        slot_done(pair0, j)
                        act.wait_ge(sgu_ready, hp * 2)
                        act.wait_ge(f_ready, 1)
                        for e in (0, 1):
                            squares_of(hp, e, bank_a)
                    if j == 10:
                        roots_of(hp, 0)
                        roots_of(hp, 1)
                    if j == 15:
                        slot_done(pair0, j)
                        act.wait_ge(qk_ready, hp * 4 + 2)
                        for e in (2, 3):
                            squares_of(hp, e, bank_b)
                    if j == 18:
                        roots_of(hp, 2)
                        roots_of(hp, 3)
                    if j - 1 in SCORE_AT:
                        exp_of(hp, SCORE_AT.index(j - 1))
                    if j == 23:
                        slot_done(pair0, j)
                        act.wait_ge(gated, hp * 2)
                        act.wait_ge(f_ready, 1)
                        for a in range(2):
                            act.activation(part[:, a, :], bank_a[:, a, :], ACT.Copy).then_inc(v_part, 1)
                    if j - 4 in SCORE_AT:
                        copy_prob_t(hp, SCORE_AT.index(j - 4))
                    if j in (25, 27):
                        a = (j - 25) // 2
                        act.wait_ge(v_turned, hp * 2 + (a + 1))
                        act.activation(v_n[:, a, :, :], bank_o[:, :].rearrange("p (i d) -> p i d", d=P),
                                       ACT.Copy).then_inc(v_ready, 1)
                    if j in (29, 35):
                        a = (j - 29) // 6
                        act.wait_ge(consts_made, CONSTS)
                        act.wait_ge(attn_sums, hp * 2 + (a + 1))
                        act.activation(mix_hi[:, bass.ds(hp * 4 + a, 1), :].rearrange("p k n -> p (k n)"),
                                       bank_o[:, :], ACT.Copy).then_inc(attn_hi, 1)
                    if j == 31:
                        slot_done(pair0, j)
                        act.wait_ge(v_turned, hp * 2 + 2)
                        for a in range(2):
                            act.activation(part[:, a, :], bank_b[:, a, :], ACT.Gelu_apprx_tanh).then_inc(vg_part, 1)
                    if j in (35, 37):
                        a = (j - 35) // 2
                        act.wait_ge(vg_agg, hp * 2 + (a + 1))
                        act.activation(vg_root[:, a, :], vg_mv[:, a, :, 1], ACT.Sqrt, bias=cols[:, 0:1]).then_inc(vg_rooted, 1)
                    if j == 39:
                        slot_done(pair0, j)
                        for a in range(2):
                            act.activation(tmp[:, a, :], bank_a[:, a, :], ACT.Gelu_apprx_tanh).then_inc(gate_ready, 1)
                        for a in range(2):
                            act.wait_ge(consts_made, CONSTS)
                            act.wait_ge(gated, hp * 2 + (a + 1))
                            act.activation(mix_hi[:, bass.ds(hp * 4 + (2 + a), 1), :], tmp[:, a:a + 1, :],
                                           ACT.Copy).then_inc(sgu_hi, 1)

            with act.Fori(0, BODIES) as b:
                pair0 = b * 2 + OUT_PAIR
                for j in range(2 * SLOTS):
                    q = j // SLOTS
                    round_slot(pair0, j + LEAD)
                    if j % SLOTS == 5:
                        for a in range(2):
                            act.wait_ge(consts_made, CONSTS)
                            act.wait_ge(stage_turned, b * 4 + (2 * q + a + 1))
                            act.activation(x1[:, bass.ds(b * 4 + (2 * q + a), 1), :], bank_s[:, a:a + 1, :],
                                           ACT.Copy).then_inc(x1_old, 1)
            act.wait_ge(sq_sums, 1)
            act.activation(inv[:, :], bank_o[:, :], ACT.Sqrt, bias=cols[:, 0:1], scale=1.0 / D).then_inc(sq_root, 1)
            with act.Fori(0, KC // 2) as t:
                for a in range(2):
                    act.wait_ge(consts_made, CONSTS)
                    act.wait_ge(h2_scaled, t * 2 + (a + 1))
                    act.activation(h_hi[:, bass.ds(t * 2 + a, 1), :], tmp[:, a:a + 1, :], ACT.Identity,
                                   bias=mod[:, bass.ds(t * 2 + (SHIFT2 + a), 1)]).then_inc(h2_hi, 1)

            def ff1_body(ch, b):
                pair0 = ch * (2 * NPAIR) + (b * 2 + FF_PAIR)
                for j in range(2 * SLOTS):
                    round_slot(pair0, j + LEAD)
                    if j % SLOTS == 7:
                        q = j // SLOTS
                        bank = (bank_a, bank_b)[q]
                        n0 = ch * KC + (b * 4 + 2 * q)
                        slot_done(pair0, j)
                        act.wait_ge(ff_ready, n0)
                        act.wait_ge(h2_ready, KC)
                        act.activation(tmp[:, :, :], bank[:, :, :], ACT.Relu).then_inc(relu_ready[q], 1)
                        for a in range(2):
                            act.wait_ge(consts_made, CONSTS)
                            act.wait_ge(ff_square, n0 + (a + 1))
                            act.activation(mix_hi[:, bass.ds(b * 4 + (2 * q + a), 1), :], tmp[:, a:a + 1, :],
                                           ACT.Copy).then_inc(ff_hi, 1)

            def copy_out(b, n):
                act.wait_ge(y_turned, n + 1)
                act.wait_ge(y_out, n * 16)
                act.activation(x_stage[:, :, :].rearrange("p i n -> p (i n)"),
                               bank_s[:, :, :].rearrange("p b n -> p (b n)"), ACT.Copy).then_inc(y_ready, 1)
                act.wait_ge(y_ready, n + 1)
                act.dma_start(out_v[:, :, bass.ds(n * PAIR, PAIR)], x_stage[:, :, :]).then_inc(y_out, 16)

            def ff2_body(ch, b, last=False, first_out=True, store=False):
                pair0 = ch * (2 * NPAIR) + (b * 2 + (FF_PAIR + NPAIR))
                for j in range(2 * SLOTS):
                    if not (last and j + LEAD >= 2 * SLOTS):
                        round_slot(pair0, j + LEAD)
                    if store and j == 3 and not first_out:
                        copy_out(b, b * 2 - 1)
                    if store and j == 11:
                        copy_out(b, b * 2)

            with act.Fori(0, FC - 1) as ch:
                with act.Fori(0, BODIES) as b:
                    ff1_body(ch, b)
                with act.Fori(0, BODIES) as b:
                    ff2_body(ch, b)
            with act.Fori(0, BODIES) as b:
                ff1_body(FC - 1, b)
            ff2_body(FC - 1, 0, store=True)
            with act.Fori(1, BODIES - 1) as b:
                ff2_body(FC - 1, b, first_out=False, store=True)
            ff2_body(FC - 1, BODIES - 1, last=True, first_out=False, store=True)
            copy_out(BODIES, NPAIR - 1)

        @block.vector
        def _(dve):
            def split_slot(pair0, j):
                n = (j % SLOTS) // 2
                dve.wait_ge(w_rounded, pair0 * SLOTS + (j + 1))
                dve.tensor_tensor(w_lo[:, j % SPLIT, :, :], raw[:, n, 2 * (j % 2):2 * (j % 2) + 2, :],
                                  w_hi[:, j % SPLIT, :, :].bitcast(F32), ALU.subtract).then_inc(w_split, 1)

            dve.memset(f_split[:, :].bitcast(F32), 0.0).then_inc(w_split, 2 * RAW)
            dve.memset(f_ones, 1.0).then_inc(f_cleared, 1)
            dve.wait_ge(rows_turned, 1)
            dve.tensor_copy(vec_b[:, :], bank_o[:, P:2 * P]).then_inc(vecs_ready, 1)
            dve.tensor_copy(vec_a[:, :], bank_o[:, 0:P]).then_inc(vecs_ready, 1)
            dve.wait_ge(vecs_ready, 2)
            dve.tensor_scalar(gq_scaled[:, :], vec_b[:, KC + G:KC + G + 1], float(DH) ** -0.5, None,
                              ALU.mult).then_inc(gq_ready, 1)
            dve.wait_ge(x_rooted, 1)
            dve.reciprocal(x_inv[:, :], x_root[:, :]).then_inc(x_inverted, 1)
            dve.wait_ge(c_ready, 1)

            with dve.Fori(0, GRPS // 2) as g2:
                for half in range(2):
                    g = g2 * 2 + half
                    for k in range(KC):
                        acc = mod_acc[:, half, :, :]
                        dve.wait_ge(mod_in[k % MRING], g * (16 * KC // MRING) + 16 * (k // MRING + 1))
                        if k == 0:
                            dve.wait_ge(mod_sums, g2 * 2 + half)
                            dve.tensor_scalar(acc, mod_tile[:, k % MRING, :, :], c_act[:, k:k + 1], None,
                                              ALU.mult).then_inc(mod_step, 1)
                        else:
                            dve.wait_ge(mod_step, g * KC + k)
                            dve.scalar_tensor_tensor(out=acc, in0=mod_tile[:, k % MRING, :, :], scalar=c_act[:, k:k + 1],
                                                     in1=acc, op0=ALU.mult, op1=ALU.add).then_inc(mod_step, 1)
                    dve.wait_ge(mod_sums, g + 1)
                    for m in range(2):
                        at = bass.ds(g * GRP + m * KC, GRP)
                        dve.tensor_tensor(mod[:, at], bank_t[:, m * GRP:(m + 1) * GRP], vec_a[:, at],
                                          ALU.add).then_inc(mod_added, 1)
                    dve.wait_ge(mod_added, g * 2 + 2)
                    dve.scalar_tensor_tensor(out=a1[:, bass.ds(g * GRP, GRP)], in0=mod[:, bass.ds(g * GRP + SCALE1, GRP)],
                                             scalar=1.0, in1=vec_a[:, bass.ds(g * GRP + 6 * KC, GRP)],
                                             op0=ALU.add, op1=ALU.mult).then_inc(a1_ready, 1)
                    dve.wait_ge(a1_ready, g + 1)
                    for t in range(GRP):
                        n = bass.ds(g * GRP + t, 1)
                        dve.wait_ge(h_hi_ready, g * GRP + (t + 1))
                        dve.tensor_scalar(xhat[:, n, :], xhat[:, n, :], a1[:, n], mod[:, n],
                                          ALU.mult, ALU.add).then_inc(h_full, 1)
                        dve.wait_ge(h_full, g * GRP + (t + 1))
                        dve.tensor_tensor(h_lo[:, n, :], xhat[:, n, :], h_hi[:, n, :].bitcast(F32),
                                          ALU.subtract).then_inc(h_ready, 1)
            dve.wait_ge(wf_rounded, 1)
            dve.tensor_tensor(wf[:, :, H:2 * H], wf_raw[:, :, :], wf[:, :, 0:H].bitcast(F32), ALU.subtract).then_inc(wf_ready, 1)
            for j in range(LEAD):
                split_slot(0, j)
            dve.wait_ge(f_copied, 1)
            dve.tensor_tensor(f_nat[:, :, :], f_two[:, :, 0:H], f_two[:, :, H:2 * H], ALU.add).then_inc(f_joined, 1)
            dve.wait_ge(f_turned, 1)
            dve.tensor_scalar(f_x, bank_o[0:H, :], bf_col[:, 0:1], None, ALU.add).then_inc(f_biased, 1)
            dve.wait_ge(f_act, 3)
            dve.scalar_tensor_tensor(out=f_x, in0=f_x, scalar=0.0, in1=f_y, op0=ALU.min, op1=ALU.subtract).then_inc(f_log, 1)
            dve.wait_ge(f_log, 1)
            dve.tensor_tensor_scan(f_cum, f_ones, f_x, 0.0, ALU.mult, ALU.add).then_inc(f_summed, 1)
            dve.wait_ge(f_summed, 1)
            dve.tensor_copy(f_split[0:H, :], f_cum).then_inc(f_hi_ready, 1)
            dve.wait_ge(f_hi_ready, 1)
            dve.tensor_tensor(f_split[32:32 + H, :], f_cum, f_split[0:H, :].bitcast(F32), ALU.subtract).then_inc(f_ready, 1)

            def norm_of(hp, e, bank):
                a = e % 2
                dve.wait_ge(norm_root, hp * 4 + (e + 1))
                dve.reciprocal(tmp[:, a, :], tmp[:, a, :]).then_inc(norm_inv, 1)
                dve.wait_ge(norm_inv, hp * 4 + (e + 1))
                dst, g = ((q_t, gq_scaled[:, 0:1]), (k_t, vec_b[:, KC + G + 1:KC + G + 2]))[e // 2]
                dve.scalar_tensor_tensor(out=dst[:, a, :], in0=bank[:, a, :], scalar=g, in1=tmp[:, a, :],
                                         op0=ALU.mult, op1=ALU.mult).then_inc(qk_ready, 1)

            def m_steps(hp, j):
                for at in range(2 * KC):
                    if (MOD_A + MOD_B)[at] != j:
                        continue
                    k = at % KC
                    dve.wait_ge(mtile_in[at % 2], hp * (16 * KC) + 16 * (at // 2 + 1))
                    if k == 0:
                        dve.wait_ge(m_sums, hp * 2 + at // KC)
                        dve.tensor_scalar(macc[:, :], mtile[:, at % 2, :], c_act[:, k:k + 1], None,
                                          ALU.mult).then_inc(m_step, 1)
                    else:
                        dve.wait_ge(m_step, hp * (2 * KC) + at)
                        dve.scalar_tensor_tensor(out=macc[:, :], in0=mtile[:, at % 2, :], scalar=c_act[:, k:k + 1],
                                                 in1=macc[:, :], op0=ALU.mult, op1=ALU.add).then_inc(m_step, 1)

            def m_add(hp, blk):
                dve.wait_ge(m_sums, hp * 2 + (blk + 1))
                at = bass.ds(hp * (2 * MBT) + (GATE1 + blk * MBT), MBT)
                dve.tensor_tensor(mod[:, at], bank_t[:, 0:MBT], vec_a[:, at], ALU.add).then_inc(m_added, 1)

            def max_of(hp, t):
                dve.wait_ge(scores, hp * 8 + (t + 1))
                dve.reduce_max(neg_max[:, t:t + 1], bank_s[:, t % 2, 0:P * (t % ST + 1)], AX_X,
                               negate=True).then_inc(maxima, 1)

            def scale_of(hp, t):
                n = P * (t % ST + 1)
                dve.wait_ge(exps, hp * 8 + (t + 1))
                dve.reciprocal(row_inv[:, t:t + 1], row_sum[:, t:t + 1]).then_inc(sums_inv, 1)
                dve.wait_ge(sums_inv, hp * 8 + (t + 1))
                dve.tensor_scalar(prob[:, t % ST, 0:n], prob[:, t % ST, 0:n], row_inv[:, t:t + 1], None,
                                  ALU.mult).then_inc(probs, 1)

            def vg_norm_stats(hp, a):
                src = (bank_t, bank_o)[a]
                dve.wait_ge(vg_turned, hp * 2 + (a + 1))
                for i in range(ST):
                    dve.bn_stats(vg_stats[:, a, i, :], src[:, P * i:P * (i + 1)]).then_inc(vg_stat, 1)
                dve.wait_ge(consts_made, CONSTS)
                dve.wait_ge(vg_stat, hp * (2 * ST) + ST * (a + 1))
                for i in range(ST):
                    ins = dve.bn_aggr(vg_mv[:, a, i, :], vg_stats[:, a, i, :])
                ins.then_inc(vg_agg, 1)

            def vg_norm(hp, a):
                src = (bank_t, bank_o)[a]
                dve.wait_ge(vg_rooted, hp * 2 + (a + 1))
                dve.reciprocal(vg_inv[:, a, :], vg_root[:, a, :]).then_inc(vg_inverted, 1)
                dve.wait_ge(vg_inverted, hp * 2 + (a + 1))
                for i in range(ST):
                    ins = dve.tensor_scalar(vg_n[:, a, i, :], src[:, P * i:P * (i + 1)], vg_mv[:, a, i, 0:1],
                                            vg_inv[:, a, i:i + 1], ALU.subtract, ALU.mult)
                ins.then_inc(vg_ready, 1)

            with dve.Fori(0, HP) as hp:
                pair0 = hp * STEP_PAIRS
                for j in range(STEP_SLOTS):
                    split_slot(pair0, j + LEAD)
                    m_steps(hp, j)
                    if j == 0:
                        dve.wait_ge(consts_made, CONSTS)
                        dve.wait_ge(scores, hp * 8)
                        dve.tensor_copy(sel_cur[:, :, :], neg_sel[:, bass.ds(hp * 2, 2)].unsqueeze(2).to_broadcast([P, 2, P])
                                        ).then_inc(sel_ready, 1)
                    if j == 4:
                        dve.wait_ge(ws_turned, hp + 1)
                        for a in range(2):
                            dve.tensor_tensor(ws_t[:, a, :], bank_t[:, P * a:P * (a + 1)], mask01[:, :], ALU.mult).then_inc(ws_ready, 1)
                    if j in (10, 12):
                        norm_of(hp, (j - 10) // 2, bank_a)
                    if j in (18, 20):
                        norm_of(hp, 2 + (j - 18) // 2, bank_b)
                    if j == 19:
                        m_add(hp, 0)
                    if j - 1 in SCORE_AT:
                        max_of(hp, SCORE_AT.index(j - 1))
                    if j - 2 in SCORE_AT:
                        scale_of(hp, SCORE_AT.index(j - 2))
                    if j in (29, 35):
                        a = (j - 29) // 6
                        dve.wait_ge(attn_hi, hp * 2 + (a + 1))
                        m = bass.ds(hp * 4 + a, 1)
                        dve.tensor_tensor(mix_lo[:, m, :].rearrange("p k n -> p (k n)"), bank_o[:, :],
                                          mix_hi[:, m, :].rearrange("p k n -> p (k n)").bitcast(F32),
                                          ALU.subtract).then_inc(attn_ready, 1)
                    if j in (35, 37):
                        vg_norm_stats(hp, (j - 35) // 2)
                    if j in (36, 38):
                        vg_norm(hp, (j - 36) // 2)
                    if j == 39:
                        dve.wait_ge(bs_in, hp * 16 + 16)
                        for a in range(2):
                            dve.wait_ge(z_sums, hp * 2 + (a + 1))
                            dve.scalar_tensor_tensor(out=part[:, a, :].rearrange("p (i t) -> p i t", t=P),
                                                     in0=bank_s[:, a, :].rearrange("p (i t) -> p i t", t=P),
                                                     scalar=vec_b[:, bass.ds(hp * 2 + (KC + a), 1)],
                                                     in1=bs_all[:, a:a + 1, :].to_broadcast([P, ST, P]),
                                                     op0=ALU.mult, op1=ALU.add).then_inc(z_ready, 1)
                    if j == 39:
                        dve.wait_ge(z_ready, hp * 2 + 2)
                        for a in range(2):
                            dve.wait_ge(gate_ready, hp * 2 + (a + 1))
                            dve.tensor_tensor(tmp[:, a, :], tmp[:, a, :], part[:, a, :], ALU.mult).then_inc(gated, 1)
                        for a in range(2):
                            m = bass.ds(hp * 4 + (2 + a), 1)
                            dve.wait_ge(sgu_hi, hp * 2 + (a + 1))
                            dve.tensor_tensor(mix_lo[:, m, :], tmp[:, a:a + 1, :], mix_hi[:, m, :].bitcast(F32),
                                              ALU.subtract).then_inc(sgu_ready, 1)
                        m_add(hp, 1)

            dve.wait_ge(gated, 2 * HP)
            dve.memset(sq_acc[:, :], 0.0).then_inc(sq_cleared, 1)
            with dve.Fori(0, BODIES) as b:
                pair0 = b * 2 + OUT_PAIR
                for j in range(2 * SLOTS):
                    split_slot(pair0, j + LEAD)
                    for at in range(KC):
                        if MOD_O[at] != j:
                            continue
                        dve.wait_ge(otile_in[at % 2], b * (8 * KC) + 16 * (at // 2 + 1))
                        if at == 0:
                            dve.wait_ge(o_sums, b)
                            dve.tensor_scalar(oacc[:, :], otile[:, at % 2, :], c_act[:, at:at + 1], None,
                                              ALU.mult).then_inc(o_step, 1)
                        else:
                            dve.wait_ge(o_step, b * KC + at)
                            dve.scalar_tensor_tensor(out=oacc[:, :], in0=otile[:, at % 2, :], scalar=c_act[:, at:at + 1],
                                                     in1=oacc[:, :], op0=ALU.mult, op1=ALU.add).then_inc(o_step, 1)
                    if j % SLOTS == 7:
                        q = j // SLOTS
                        bank = (bank_a, bank_b)[q]
                        dve.wait_ge(slot_used, pair0 * SLOTS + (j + 1 + SPLIT))
                        dve.wait_ge(m_added, 2 * HP)
                        for a in range(2):
                            n = bass.ds(b * 4 + (2 * q + a), 1)
                            dve.wait_ge(x1_old, b * 4 + (2 * q + a + 1))
                            dve.scalar_tensor_tensor(out=x1[:, n, :], in0=bank[:, a:a + 1, :],
                                                     scalar=mod[:, bass.ds(b * 4 + (GATE1 + 2 * q + a), 1)],
                                                     in1=x1[:, n, :], op0=ALU.mult, op1=ALU.add).then_inc(x1_ready[q], 1)
                        for a in range(2):
                            n = bass.ds(b * 4 + (2 * q + a), 1)
                            dve.wait_ge(x1_ready[q], b * 2 + (a + 1))
                            dve.tensor_tensor(tmp[:, a:a + 1, :], x1[:, n, :], x1[:, n, :], ALU.mult).then_inc(x1_square, 1)
                            dve.wait_ge(x1_square, b * 4 + (2 * q + a + 1))
                            dve.wait_ge(sq_added, b * 4 + (2 * q + a))
                            dve.wait_ge(sq_cleared, 1)
                            dve.tensor_tensor(sq_acc[:, :], sq_acc[:, :], tmp[:, a, :], ALU.add).then_inc(sq_added, 1)
                    if j == 15:
                        dve.wait_ge(o_sums, b + 1)
                        at = bass.ds(b * MOT + GATE2, MOT)
                        dve.tensor_tensor(mod[:, at], bank_t[:, 0:MOT], vec_a[:, at], ALU.add).then_inc(o_added, 1)
            dve.scalar_tensor_tensor(out=a2[:, :], in0=mod[:, SCALE2:SCALE2 + KC], scalar=1.0,
                                     in1=vec_a[:, 7 * KC:8 * KC], op0=ALU.add, op1=ALU.mult).then_inc(a2_ready, 1)
            dve.wait_ge(sq_root, 1)
            dve.reciprocal(inv[:, :], inv[:, :]).then_inc(inv_ready, 1)
            dve.wait_ge(inv_ready, 1)
            dve.wait_ge(a2_ready, 1)
            with dve.Fori(0, KC // 2) as t:
                for a in range(2):
                    dve.wait_ge(h2_ready, t * 2)
                    dve.scalar_tensor_tensor(out=tmp[:, a, :], in0=x1[:, bass.ds(t * 2 + a, 1), :].rearrange("p k n -> p (k n)"),
                                             scalar=a2[:, bass.ds(t * 2 + a, 1)], in1=inv[:, :],
                                             op0=ALU.mult, op1=ALU.mult).then_inc(h2_scaled, 1)
                for a in range(2):
                    n = bass.ds(t * 2 + a, 1)
                    dve.wait_ge(h2_hi, t * 2 + (a + 1))
                    dve.scalar_tensor_tensor(out=h_lo[:, n, :], in0=tmp[:, a:a + 1, :],
                                             scalar=mod[:, bass.ds(t * 2 + (SHIFT2 + a), 1)],
                                             in1=h_hi[:, n, :].bitcast(F32), op0=ALU.add, op1=ALU.subtract).then_inc(h2_ready, 1)

            def ff1_body(ch, b):
                pair0 = ch * (2 * NPAIR) + (b * 2 + FF_PAIR)
                for j in range(2 * SLOTS):
                    split_slot(pair0, j + LEAD)
                    if j % SLOTS == 7:
                        q = j // SLOTS
                        n0 = ch * KC + (b * 4 + 2 * q)
                        dve.wait_ge(relu_ready[q], ch * BODIES + (b + 1))
                        for a in range(2):
                            dve.tensor_tensor(tmp[:, a, :], tmp[:, a, :], tmp[:, a, :], ALU.mult).then_inc(ff_square, 1)
                        for a in range(2):
                            m = bass.ds(b * 4 + (2 * q + a), 1)
                            dve.wait_ge(ff_hi, n0 + (a + 1))
                            dve.tensor_tensor(mix_lo[:, m, :], tmp[:, a:a + 1, :], mix_hi[:, m, :].bitcast(F32),
                                              ALU.subtract).then_inc(ff_ready, 1)

            def ff2_body(ch, b, last=False, final=False):
                pair0 = ch * (2 * NPAIR) + (b * 2 + (FF_PAIR + NPAIR))
                for j in range(2 * SLOTS):
                    if not (last and j + LEAD >= 2 * SLOTS):
                        split_slot(pair0, j + LEAD)
                    if j % SLOTS == 7:
                        q = j // SLOTS
                        bank = (bank_a, bank_b)[q]
                        dve.wait_ge(slot_used, pair0 * SLOTS + (j + 1 + SPLIT))
                        if final:
                            dve.wait_ge(y_turned, b * 2 + q)
                        for a in range(2):
                            n = bass.ds(b * 4 + (2 * q + a), 1)
                            dve.scalar_tensor_tensor(out=part[:, a:a + 1, :] if final else x1[:, n, :],
                                                     in0=bank[:, a:a + 1, :],
                                                     scalar=mod[:, bass.ds(b * 4 + (GATE2 + 2 * q + a), 1)],
                                                     in1=x1[:, n, :], op0=ALU.mult, op1=ALU.add).then_inc(ff_added[q], 1)

            dve.wait_ge(o_added, BODIES)
            with dve.Fori(0, FC - 1) as ch:
                with dve.Fori(0, BODIES) as b:
                    ff1_body(ch, b)
                with dve.Fori(0, BODIES) as b:
                    ff2_body(ch, b)
            with dve.Fori(0, BODIES) as b:
                ff1_body(FC - 1, b)
            with dve.Fori(0, BODIES - 1) as b:
                ff2_body(FC - 1, b, final=True)
            ff2_body(FC - 1, BODIES - 1, last=True, final=True)

        @block.tensor
        def _(pe):
            def product(dst, w_slot, kk, a, act_k, hi, lo, first, last):
                wh = w_hi[:, w_slot, kk, P * a:P * (a + 1)]
                wl = w_lo[:, w_slot, kk, P * a:P * (a + 1)]
                pe.matmul(dst, lhsT=wh, rhs=hi[:, act_k, :], start=first, stop=False)
                pe.matmul(dst, lhsT=wh, rhs=lo[:, act_k, :], start=False, stop=False)
                return pe.matmul(dst, lhsT=wl, rhs=hi[:, act_k, :], start=False, stop=last)

            def slot(pair0, j, bank, hi, lo):
                pe.wait_ge(w_split, pair0 * SLOTS + (j + 1 + 2 * RAW))
                for kk in range(2):
                    k = 2 * (j % SLOTS) + kk
                    for a in range(2):
                        ins = product(bank[:, a, :], j % SPLIT, kk, a, k, hi, lo, k == 0, k == KC - 1)
                ins.then_inc(slot_used, 1)

            pe.wait_ge(consts_made, CONSTS)
            pe.wait_ge(rows_in, 16 * 7)
            pe.transpose(bank_o[:, P:2 * P], rows_b[:, :], ident[:, :]).then_inc(slot_used, SPLIT)
            pe.transpose(bank_o[:, 0:P], rows_a[:, :], ident[:, :]).then_inc(rows_turned, 1)
            pe.wait_ge(x_normed, ST)
            for t in range(KC):
                if t >= 2:
                    pe.wait_ge(xhat_ready, t - 1)
                for i in range(ST):
                    ins = pe.transpose(bank_s[:, t % 2, P * i:P * (i + 1)], x_nat[:, i, P * t:P * (t + 1)], ident[:, :])
                ins.then_inc(x_turned, 1)

            def column_sums(acc, n, dst):
                for t in range(n):
                    ins = pe.matmul(dst[:, t:t + 1], lhsT=acc[:, P * t:P * (t + 1)], rhs=ones[:, 0:1], start=True, stop=True)
                return ins

            with pe.Fori(0, GRPS // 2) as g2:
                for half in range(2):
                    pe.wait_ge(mod_step, g2 * (2 * KC) + (half + 1) * KC)
                    pe.wait_ge(mod_added, g2 * 4 + 2 * half)
                    for m in range(2):
                        ins = column_sums(mod_acc[:, half, m, :], GRP, bank_t[:, m * GRP:(m + 1) * GRP])
                    ins.then_inc(mod_sums, 1)

            pe.wait_ge(wf_ready, 1)
            pe.wait_ge(h_ready, KC)
            for i in range(ST):
                for k in range(KC):
                    for act_h in (h_hi, h_lo):
                        ins = pe.matmul(bank_o[:, 2 * H * i:2 * H * (i + 1)], lhsT=act_h[:, k, P * i:P * (i + 1)], rhs=wf[:, k, :],
                                        start=(k == 0 and act_h is h_hi), stop=(k == KC - 1 and act_h is h_lo))
            ins.then_inc(f_sums, 1)

            pe.wait_ge(f_joined, 1)
            for i in range(ST):
                ins = pe.matmul(bank_o[0:H, P * i:P * (i + 1)], lhsT=f_nat[:, i, :], rhs=ident[:, :], start=True, stop=True)
            ins.then_inc(f_turned, 1)

            def head_slot_tasks(hp, j):
                if j == 3:
                    pe.wait_ge(ws_in, hp * 16 + 16)
                    pe.wait_ge(m_added, hp * 2)
                    for a in range(2):
                        ins = pe.transpose(bank_t[:, P * a:P * (a + 1)], ws_nat[:, a, :], ident[:, :])
                    ins.then_inc(ws_turned, 1)
                if j in (9, 17):
                    for a in range(2):
                        e = 2 * (j // SLOTS - 1) + a
                        pe.wait_ge(squares, hp * 4 + (e + 1))
                        if e == 0:
                            pe.wait_ge(z_ready, hp * 2)
                        if e == 2:
                            pe.wait_ge(ws_ready, hp * 2 + 2)
                        if e == 3:
                            pe.wait_ge(vg_ready, hp * 2)
                            pe.wait_ge(f_biased, 1)
                        dst = (bank_s[:, 0, :], bank_s[:, 1, :], bank_t[:, :], bank_o[:, :])[e]
                        pe.matmul(dst, lhsT=ones[:, :], rhs=tmp[:, a, :], start=True, stop=True).then_inc(norm_sums, 1)
                if j == 18:
                    pe.wait_ge(norm_root, hp * 4 + 3)
                    pe.wait_ge(m_step, hp * (2 * KC) + KC)
                    column_sums(macc, MBT, bank_t).then_inc(m_sums, 1)
                if j in SCORE_AT:
                    t = SCORE_AT.index(j)
                    a, i = t // ST, t % ST
                    n = P * (i + 1)
                    dst = bank_s[:, t % 2, :]
                    pe.wait_ge(qk_ready, hp * 4 + (3 + a))
                    if t < 2:
                        pe.wait_ge(norm_root, hp * 4 + 2)
                    else:
                        pe.wait_ge(exps, hp * 8 + (t - 1))
                    if t == 0:
                        pe.wait_ge(sel_ready, hp + 1)
                        pe.wait_ge(f_ready, 1)
                    pe.matmul(dst[:, 0:n], lhsT=q_t[:, a, P * i:P * (i + 1)], rhs=k_t[:, a, 0:n], start=True, stop=False)
                    pe.matmul(dst[:, 0:n], lhsT=sel_cur[:, a, :], rhs=f_split[:, 0:n], start=False, stop=False)
                    pe.matmul(dst[:, P * i:n], lhsT=ident_bf[:, :], rhs=mask_bf[:, :], start=False, stop=True).then_inc(scores, 1)
                if j in (24, 26):
                    a = (j - 24) // 2
                    pe.wait_ge(v_part, hp * 2 + (a + 1))
                    if a == 0:
                        pe.wait_ge(norm_root, hp * 4 + 4)
                    else:
                        pe.wait_ge(v_ready, hp * 2 + 1)
                    for i in range(ST):
                        ins = pe.transpose(bank_o[:, P * i:P * (i + 1)], part[:, a, P * i:P * (i + 1)], ident[:, :])
                    ins.then_inc(v_turned, 1)
                if j - 3 in SCORE_AT:
                    t = SCORE_AT.index(j - 3)
                    i = t % ST
                    pe.wait_ge(probs, hp * 8 + (t + 1))
                    if t == 0:
                        pe.wait_ge(m_added, hp * 2 + 1)
                    else:
                        pe.wait_ge(probs_t, hp * 8 + t)
                    for jj in range(i + 1):
                        ins = pe.transpose(bank_t[:, P * jj:P * (jj + 1)], prob[:, i, P * jj:P * (jj + 1)], ident[:, :])
                    ins.then_inc(probs_turned, 1)
                if j in (28, 34):
                    a = (j - 28) // 6
                    pe.wait_ge(probs_t, hp * 8 + ST * (a + 1))
                    if a == 0:
                        pe.wait_ge(v_ready, hp * 2 + 2)
                    else:
                        pe.wait_ge(attn_ready, hp * 2 + 1)
                    for i in range(ST):
                        ins = pe.matmul(bank_o[:, P * i:S], lhsT=v_n[:, a, i, :], rhs=prob_t[:, i, P * i:S],
                                        start=(i == 0), stop=(i == ST - 1))
                    ins.then_inc(attn_sums, 1)
                if j in (35, 36):
                    a = j - 35
                    dst = (bank_t, bank_o)[a]
                    pe.wait_ge(vg_part, hp * 2 + (a + 1))
                    if a == 0:
                        pe.wait_ge(probs_t, hp * 8 + 8)
                    else:
                        pe.wait_ge(attn_ready, hp * 2 + 2)
                    for i in range(ST):
                        ins = pe.transpose(dst[:, P * i:P * (i + 1)], part[:, a, P * i:P * (i + 1)], ident[:, :])
                    ins.then_inc(vg_turned, 1)
                if j == 39:
                    pe.wait_ge(vg_ready, hp * 2 + 1)
                    pe.wait_ge(m_step, hp * (2 * KC) + 2 * KC)
                    column_sums(macc, MBT, bank_t).then_inc(m_sums, 1)
                if j in (38, 39):
                    a = j - 38
                    pe.wait_ge(vg_ready, hp * 2 + (a + 1))
                    pe.wait_ge(ws_ready, hp * 2 + 2)
                    if a == 0:
                        pe.wait_ge(exps, hp * 8 + 8)
                    for i in range(ST):
                        ins = pe.matmul(bank_s[:, a, P * i:P * (i + 1)], lhsT=vg_n[:, a, i, :], rhs=ws_t[:, a, :],
                                        start=True, stop=True)
                    ins.then_inc(z_sums, 1)

            with pe.Fori(0, HP) as hp:
                for j in range(STEP_SLOTS):
                    if j == 0:
                        pe.wait_ge(gate_ready, hp * 2)
                    if j == SLOTS:
                        pe.wait_ge(vg_part, hp * 2)
                    if j == 2 * SLOTS:
                        pe.wait_ge(qk_ready, hp * 4 + 2)
                    if j == 3 * SLOTS:
                        pe.wait_ge(qk_ready, hp * 4 + 4)
                    if j == 4 * SLOTS:
                        pe.wait_ge(v_part, hp * 2 + 2)
                    slot(hp * STEP_PAIRS, j, (bank_a, bank_b)[(j // SLOTS) % 2], h_hi, h_lo)
                    head_slot_tasks(hp, j)

            with pe.Fori(0, BODIES) as b:
                for j in range(2 * SLOTS):
                    q = j // SLOTS
                    if j % SLOTS == 0:
                        pe.wait_ge((gate_ready, vg_part)[q], HP * 2)
                        pe.wait_ge(x1_ready[q], b * 2)
                    if q == 0:
                        pe.wait_ge((attn_ready, sgu_ready)[j % 2], 2 * (j // 2 + 1))
                    slot(b * 2 + OUT_PAIR, j, (bank_a, bank_b)[q], mix_hi, mix_lo)
                    if j % SLOTS == 3:
                        pe.wait_ge(stage_in, b * 32 + 16 * (q + 1))
                        pe.wait_ge(z_ready, HP * 2)
                        pe.wait_ge(x1_old, b * 4 + 2 * q)
                        for a in range(2):
                            for i in range(ST):
                                ins = pe.transpose(bank_s[:, a, P * i:P * (i + 1)], x_stage[:, i, P * a:P * (a + 1)], ident[:, :])
                            ins.then_inc(stage_turned, 1)
                    if j == 14:
                        pe.wait_ge(m_added, HP * 2)
                        pe.wait_ge(o_added, b)
                        pe.wait_ge(o_step, b * KC + KC)
                        column_sums(oacc, MOT, bank_t).then_inc(o_sums, 1)
            pe.wait_ge(sq_added, KC)
            pe.wait_ge(vg_ready, HP * 2)
            pe.matmul(bank_o[:, :], lhsT=ones[:, :], rhs=sq_acc[:, :], start=True, stop=True).then_inc(sq_sums, 1)

            def ff1_body(ch, b):
                for j in range(2 * SLOTS):
                    q = j // SLOTS
                    if j % SLOTS == 0:
                        pe.wait_ge(x1_ready[q], 2 * BODIES)
                        pe.wait_ge(relu_ready[q], ch * BODIES + b)
                        pe.wait_ge(ff_added[q], ch * (2 * BODIES))
                    if q == 0:
                        pe.wait_ge(h2_ready, 2 * j + 2)
                    slot(ch * (2 * NPAIR) + (b * 2 + FF_PAIR), j, (bank_a, bank_b)[q], h_hi, h_lo)

            def turn_out(b, n):
                q = 1 if n is None else 0
                pair = b * 2 + q
                pe.wait_ge(ff_added[q], (FC - 1) * 2 * BODIES + (b * 2 + 2))
                pe.wait_ge(y_ready, pair)
                flat = bank_s[:, :, :].rearrange("p b n -> p (b n)")
                for i in range(ST):
                    for a in range(2):
                        at = PAIR * i + P * a
                        ins = pe.transpose(flat[:, at:at + P], part[:, a, P * i:P * (i + 1)], ident[:, :])
                ins.then_inc(y_turned, 1)

            def ff2_body(ch, b, final=False, first=False):
                for j in range(2 * SLOTS):
                    q = j // SLOTS
                    if j % SLOTS == 0:
                        pe.wait_ge(relu_ready[q], ch * BODIES + BODIES)
                        pe.wait_ge(ff_added[q], ch * (2 * BODIES) + b * 2)
                    if q == 0:
                        pe.wait_ge(ff_ready, ch * KC + (2 * j + 2))
                    slot(ch * (2 * NPAIR) + (b * 2 + (FF_PAIR + NPAIR)), j, (bank_a, bank_b)[q], mix_hi, mix_lo)
                    if final and not first and j == 2:
                        turn_out(b - 1, None)
                    if final and j == 10:
                        turn_out(b, 0)

            with pe.Fori(0, FC - 1) as ch:
                with pe.Fori(0, BODIES) as b:
                    ff1_body(ch, b)
                with pe.Fori(0, BODIES) as b:
                    ff2_body(ch, b)
            with pe.Fori(0, BODIES) as b:
                ff1_body(FC - 1, b)
            ff2_body(FC - 1, 0, final=True, first=True)
            with pe.Fori(1, BODIES) as b:
                ff2_body(FC - 1, b, final=True)
            turn_out(BODIES - 1, None)


_INS = ["x", "c", "w_ada", "b_ada", "g_mix", "w_in", "b_f", "g_q", "g_k", "g_sgu", "w_s", "b_s",
        "w_out", "g_ffn", "w_ff1", "w_ff2"]


def kernel(**inputs):
    import numpy as np
    import concourse.bacc as bacc
    from concourse.bass_utils import run_bass_kernel_spmd

    nc = bacc.Bacc("TRN2", target_bir_lowering=False, num_devices=1, dynamic_dma_scratch_size=1024)
    arrays, args = {}, []
    for name in _INS:
        a = np.ascontiguousarray(inputs[name])
        arrays[f"in_{name}"] = a
        args.append(nc.dram_tensor(f"in_{name}", a.shape, mybir.dt.from_np(a.dtype), kind="ExternalInput").ap())
    shape = arrays["in_x"].shape
    out = nc.dram_tensor("out_0", shape, F32, kind="ExternalOutput").ap()
    block_program(nc, *args, out)
    r = run_bass_kernel_spmd(nc, [arrays], core_ids=[0])
    return r.results[0]["out_0"]
```

```python
from contextlib import ExitStack

import concourse.bass as bass
from concourse import mybir

P = 128
F32 = mybir.dt.float32
F32R = mybir.dt.float32r
BF16 = mybir.dt.bfloat16
ALU = mybir.AluOpType
ACT = mybir.ActivationFunctionType
AX_X = mybir.AxisListType.X
EPS = 1e-6
NEG = -1.0e30


def block_program(nc, x, c, w_ada, b_ada, g_mix, w_in, b_f, g_q, g_k, g_sgu, w_s, b_s,
                  w_out, g_ffn, w_ff1, w_ff2, out):
    _, S, D = x.shape
    H = b_f.shape[1]
    G = g_sgu.shape[1]
    DH = g_q.shape[1]
    AW = H * DH
    GW = G * P
    DFF = w_ff1.shape[2]
    KC = D // P
    ST = S // P
    HP = H // 2
    FC = DFF // D
    PAIR = 2 * P
    SLOTS = KC // 2
    NPAIR = D // PAIR
    BODIES = NPAIR // 2
    LEAD = 3
    STEP_PAIRS = 5
    STEP_SLOTS = STEP_PAIRS * SLOTS
    OUT_PAIR = HP * STEP_PAIRS
    FF_PAIR = OUT_PAIR + NPAIR
    CONSTS = 12
    START = 1
    RAW = 4
    SPLIT = 4
    assert (S, KC, ST, DH, H, G, AW, GW) == (512, 16, 4, P, G, H, GW, AW) and FC == 4

    COL_K, COL_V, COL_F = AW, 2 * AW, 3 * AW
    COL_U = COL_F + H
    COL_VG = COL_U + GW
    SHIFT1, SCALE1, GATE1, SHIFT2, SCALE2, GATE2 = (n * KC for n in range(6))

    GRP = 4
    GRPS = KC // GRP
    GC = GRP * P
    MRING = 8
    ABT = 4
    AB = ABT * P
    ARING = 4
    OUT_BLOCK = 2 * HP
    FF_BLOCK = OUT_BLOCK + BODIES
    ADA_IN = [2, 3, 4, 5, 6, 7, 8, 9, 11, 13, 14, 15, 16, 17, 17, 19,
              22, 23, 24, 25, 26, 27, 28, 29, 30, 30, 31, 32, 33, 34, 35, 36]
    ADA_BODY = [2, 3, 4, 5, 6, 8, 8, 9, 9, 10, 10, 11, 12, 12, 13, 13]
    SCORE_AT = [20, 21, 22, 23, 26, 27, 28, 29]
    assert len(ADA_IN) == 2 * KC and len(ADA_BODY) == KC and FF_BLOCK * ABT == GATE2 - GATE1

    with ExitStack() as ctx:
        def sb(name, shape, dt=F32, where=ctx):
            return where.enter_context(nc.sbuf_tensor(name, shape, dt))

        def sem(name):
            return ctx.enter_context(nc.semaphore(name))

        bank_a = ctx.enter_context(nc.psum_tensor("bank_a", [P, 2, S], F32))
        bank_b = ctx.enter_context(nc.psum_tensor("bank_b", [P, 2, S], F32))
        bank_s = ctx.enter_context(nc.psum_tensor("bank_s", [P, 2, S], F32))
        bank_t = ctx.enter_context(nc.psum_tensor("bank_t", [P, S], F32))
        bank_o = ctx.enter_context(nc.psum_tensor("bank_o", [P, S], F32))

        ident = sb("ident", [P, P])
        ident_bf = sb("ident_bf", [P, P], BF16)
        mask_bf = sb("mask_bf", [P, P], BF16)
        mask01 = sb("mask01", [P, P])
        ones = sb("ones", [P, P])
        cols = sb("cols", [P, 2])
        vec_a = sb("vec_a", [P, P])
        vec_b = sb("vec_b", [P, P])
        c_act = sb("c_act", [P, KC])
        gq_scaled = sb("gq_scaled", [P, 1])
        bf_col = sb("bf_col", [H, 1])
        mod = sb("mod", [P, 6 * KC])
        a1 = sb("a1", [P, KC])
        a2 = sb("a2", [P, KC])
        x_sum = sb("x_sum", [P, ST])
        x_root = sb("x_root", [P, ST])
        x_inv = sb("x_inv", [P, ST])
        neg_sel = sb("neg_sel", [P, H])
        f_split = sb("f_split", [P, S], F32R)
        wf_raw = sb("wf_raw", [P, KC, H])
        wf = sb("wf", [P, KC, 2 * H], F32R)
        f_two = sb("f_two", [P, ST, 2 * H])
        f_nat = sb("f_nat", [P, ST, H])
        neg_max = sb("neg_max", [P, 8])
        row_sum = sb("row_sum", [P, 8])
        row_inv = sb("row_inv", [P, 8])
        vg_stats = sb("vg_stats", [P, 2, ST, 6])
        vg_mv = sb("vg_mv", [P, 2, ST, 2])
        vg_log = sb("vg_log", [P, 2, ST])
        vg_inv = sb("vg_inv", [P, 2, ST])
        raw = sb("raw", [P, RAW, 4, PAIR])
        w_hi = sb("w_hi", [P, SPLIT, 2, PAIR], F32R)
        w_lo = sb("w_lo", [P, SPLIT, 2, PAIR], F32R)
        h_hi = sb("h_hi", [P, KC, S], F32R)
        early = ExitStack()
        xhat = sb("xhat", [P, KC, S], F32, early)
        early.close()
        h_lo = sb("h_lo", [P, KC, S], F32R)
        early = ExitStack()
        mod_tile = sb("mod_tile", [P, MRING, 2, GC], F32, early)
        mod_acc = sb("mod_acc", [P, 2, GC], F32, early)
        early.close()
        mix_hi = sb("mix_hi", [P, KC, S], F32R)
        mix_lo = sb("mix_lo", [P, KC, S], F32R)
        tmp = sb("tmp", [P, 2, S])
        part = sb("part", [P, 2, S])
        early = ExitStack()
        x_nat = sb("x_nat", [P, ST, D], F32, early)
        early.close()
        early = ExitStack()
        q_t = sb("q_t", [P, 2, S], F32, early)
        k_t = sb("k_t", [P, 2, S], F32, early)
        v_n = sb("v_n", [P, 2, ST, P], F32, early)
        vg_n = sb("vg_n", [P, 2, ST, P], F32, early)
        prob = sb("prob", [P, ST, S], F32, early)
        prob_t = sb("prob_t", [P, ST, S], F32, early)
        early.close()
        x1 = sb("x1", [P, KC, S])
        early = ExitStack()
        rows_a = sb("rows_a", [P, P], F32, early)
        rows_b = sb("rows_b", [P, P], F32, early)
        early.close()
        early = ExitStack()
        ws_nat = sb("ws_nat", [P, 2, P], F32, early)
        ws_t = sb("ws_t", [P, 2, P], F32, early)
        bs_all = sb("bs_all", [P, 2, P], F32, early)
        sel_cur = sb("sel_cur", [P, 2, P], F32R, early)
        early.close()
        x_stage = sb("x_stage", [P, ST, PAIR])
        ada_tile = sb("ada_tile", [P, ARING, AB])
        ada_acc = sb("ada_acc", [P, AB])
        inv, sq_acc = part[:, 0, :], part[:, 1, :]
        f_x, f_y = tmp[0:H, 0, :], tmp[0:H, 1, :]
        f_cum, f_ones = part[0:H, 0, :], part[0:H, 1, :]

        consts_made = sem("consts_made")
        rows_in = sem("rows_in")
        small_in = sem("small_in")
        rows_turned = sem("rows_turned")
        vecs_ready = sem("vecs_ready")
        c_ready = sem("c_ready")
        gq_ready = sem("gq_ready")
        x_in = [sem(f"x_in{i}") for i in range(ST)]
        x_squared = sem("x_squared")
        x_rooted = sem("x_rooted")
        x_inverted = sem("x_inverted")
        x_normed = sem("x_normed")
        x_turned = sem("x_turned")
        xhat_ready = sem("xhat_ready")
        mod_in = [sem(f"mod_in{i}") for i in range(MRING)]
        mod_step = sem("mod_step")
        mod_sums = sem("mod_sums")
        mod_added = sem("mod_added")
        a1_ready = sem("a1_ready")
        h_full = sem("h_full")
        h_hi_ready = sem("h_hi_ready")
        h_ready = sem("h_ready")
        wf_rounded = sem("wf_rounded")
        wf_ready = sem("wf_ready")
        f_sums = sem("f_sums")
        f_biased = sem("f_biased")
        f_act = sem("f_act")
        f_log = sem("f_log")
        f_summed = sem("f_summed")
        f_hi_ready = sem("f_hi_ready")
        f_ready = sem("f_ready")
        f_cleared = sem("f_cleared")
        raw_in = [sem(f"raw_in{i}") for i in range(RAW)]
        w_rounded = sem("w_rounded")
        w_split = sem("w_split")
        slot_used = sem("slot_used")
        ws_in = sem("ws_in")
        bs_in = sem("bs_in")
        ws_turned = sem("ws_turned")
        ws_ready = sem("ws_ready")
        sel_ready = sem("sel_ready")
        squares = sem("squares")
        norm_sums = sem("norm_sums")
        norm_root = sem("norm_root")
        norm_inv = sem("norm_inv")
        qk_ready = sem("qk_ready")
        scores = sem("scores")
        maxima = sem("maxima")
        exps = sem("exps")
        sums_inv = sem("sums_inv")
        probs = sem("probs")
        probs_turned = sem("probs_turned")
        probs_t = sem("probs_t")
        v_part = sem("v_part")
        v_turned = sem("v_turned")
        v_ready = sem("v_ready")
        attn_sums = sem("attn_sums")
        attn_hi = sem("attn_hi")
        attn_ready = sem("attn_ready")
        vg_part = sem("vg_part")
        vg_turned = sem("vg_turned")
        vg_stat = sem("vg_stat")
        vg_agg = sem("vg_agg")
        vg_logged = sem("vg_logged")
        vg_inverted = sem("vg_inverted")
        vg_ready = sem("vg_ready")
        z_sums = sem("z_sums")
        z_ready = sem("z_ready")
        gate_ready = sem("gate_ready")
        gated = sem("gated")
        sgu_hi = sem("sgu_hi")
        sgu_ready = sem("sgu_ready")
        ada_in = [sem(f"ada_in{i}") for i in range(ARING)]
        ada_step = sem("ada_step")
        ada_sums = sem("ada_sums")
        ada_added = sem("ada_added")
        stage_in = sem("stage_in")
        stage_turned = sem("stage_turned")
        x1_old = sem("x1_old")
        x1_ready = [sem(f"x1_ready{q}") for q in range(2)]
        x1_square = sem("x1_square")
        sq_added = sem("sq_added")
        sq_sums = sem("sq_sums")
        f_turned = sem("f_turned")
        f_copied = sem("f_copied")
        f_joined = sem("f_joined")
        sq_root = sem("sq_root")
        sq_cleared = sem("sq_cleared")
        inv_ready = sem("inv_ready")
        a2_ready = sem("a2_ready")
        h2_scaled = sem("h2_scaled")
        h2_hi = sem("h2_hi")
        h2_ready = sem("h2_ready")
        relu_ready = [sem(f"relu_ready{q}") for q in range(2)]
        ff_square = sem("ff_square")
        ff_hi = sem("ff_hi")
        ff_ready = sem("ff_ready")
        ff_added = [sem(f"ff_added{q}") for q in range(2)]
        y_turned = sem("y_turned")
        y_ready = sem("y_ready")
        y_out = sem("y_out")

        w_in_v = w_in[0].rearrange("(k p) n -> p k n", p=P)
        w_out_v = w_out[0].rearrange("(g h c p) n -> p h g c n", g=2, h=HP, p=P)
        w_ff1_v = w_ff1[0].rearrange("(k p) n -> p k n", p=P)
        w_ff2_v = w_ff2[0].rearrange("(c k p) n -> p c k n", c=FC, p=P)
        ada_v = w_ada[0].rearrange("(k p) (m n) -> k p m n", p=P, m=6)
        ada_flat = w_ada[0].rearrange("(k p) n -> k p n", p=P)
        x_v = x[0].rearrange("(i p) d -> p i d", p=P)
        out_v = out[0].rearrange("(i p) d -> p i d", p=P)
        b_s_v = b_s[0].rearrange("g t -> (g t)")
        f_banks = [bank_s[:, 0, :], bank_s[:, 1, :], bank_o[:, :], bank_b[:, 0, :]]

        block = ctx.enter_context(nc.Block())

        @block.sync
        def _(sp):
            sp.wait_ge(consts_made, 6)
            sp.dma_start(rows_b[0:KC, :], c.rearrange("a (k p) -> (a k) p", p=P)).then_inc(rows_in, 16)
            sp.dma_start(rows_a[0:6 * KC, :], b_ada.rearrange("a (k p) -> (a k) p", p=P)).then_inc(rows_in, 16)
            sp.dma_start(rows_a[6 * KC:7 * KC, :], g_mix.rearrange("a (k p) -> (a k) p", p=P)).then_inc(rows_in, 16)
            sp.dma_start(rows_a[7 * KC:8 * KC, :], g_ffn.rearrange("a (k p) -> (a k) p", p=P)).then_inc(rows_in, 16)
            sp.dma_start(rows_b[KC:KC + G, :], g_sgu[0]).then_inc(rows_in, 16)
            sp.dma_start(rows_b[KC + G:KC + G + 1, :], g_q).then_inc(rows_in, 16)
            sp.dma_start(rows_b[KC + G + 1:KC + G + 2, :], g_k).then_inc(rows_in, 16)
            for i in range(ST):
                sp.dma_start(x_nat[:, i, :], x_v[:, i, :]).then_inc(x_in[i], 16)

            sp.dma_start(bf_col[:, :], b_f.rearrange("a h -> h a")).then_inc(small_in, 16)
            sp.dma_start(wf_raw[:, :, :], w_in_v[:, :, COL_F:COL_F + H]).then_inc(small_in, 16)

            def mod_load(g, k):
                sp.dma_start(mod_tile[:, k % MRING, :, :],
                             ada_v[k, :, 0:2, bass.ds(g * GC, GC)]).then_inc(mod_in[k % MRING], 16)

            for k in range(MRING):
                mod_load(0, k)
            for k in range(MRING, KC):
                sp.wait_ge(mod_step, k - MRING + 1)
                mod_load(0, k)
            with sp.Fori(1, GRPS) as g:
                for k in range(KC):
                    sp.wait_ge(mod_step, g * KC + (k - MRING + 1))
                    mod_load(g, k)
            def chunk_load(pair, n, src):
                sp.wait_ge(w_split, pair * SLOTS + 2 * n + 2)
                sp.dma_start(raw[:, n, :, :], src).then_inc(raw_in[n], 32)

            with sp.Fori(0, HP) as hp:
                for j in range(STEP_SLOTS):
                    if j % 2 == 0:
                        col = (0, COL_K, COL_V, COL_VG, COL_U)[j // SLOTS]
                        n = (j % SLOTS) // 2
                        chunk_load(hp * STEP_PAIRS + j // SLOTS, n,
                                   w_in_v[:, 4 * n:4 * n + 4, bass.ds(hp * PAIR + col, PAIR)])
                    if j == 1:
                        sp.wait_ge(ws_turned, START + hp)
                        sp.dma_start(ws_nat[:, :, :], w_s[0].rearrange("g t s -> t g s")[:, bass.ds(hp * 2, 2), :]).then_inc(ws_in, 16)
                    if j == 4:
                        sp.wait_ge(z_ready, START + hp * 2)
                        sp.dma_start(bs_all[:, :, :].rearrange("p g t -> p (g t)"),
                                     b_s_v[bass.ds(hp * PAIR, PAIR)].partition_broadcast(P)).then_inc(bs_in, 16)
            with sp.Fori(0, BODIES) as b:
                for q in range(2):
                    for n in range(4):
                        sp.wait_ge(w_split, (b * 2 + (OUT_PAIR + q)) * SLOTS + 2 * n + 2)
                        for g in range(2):
                            sp.dma_start(raw[:, n, 2 * g:2 * g + 2, :],
                                         w_out_v[:, n, g, :, bass.ds(b * (2 * PAIR) + q * PAIR, PAIR)]).then_inc(raw_in[n], 16)
                        if n == 2:
                            sp.wait_ge(stage_turned, START + b * 4 + 2 * q)
                            sp.wait_ge(scores, START + 8 * HP)
                            sp.wait_ge(z_ready, START + 2 * HP)
                            sp.dma_start(x_stage[:, :, :],
                                         x_v[:, :, bass.ds(b * (2 * PAIR) + q * PAIR, PAIR)]).then_inc(stage_in, 16)

            def ff1_loads(ch, b):
                for q in range(2):
                    for n in range(4):
                        chunk_load(ch * (2 * NPAIR) + (b * 2 + (FF_PAIR + q)), n,
                                   w_ff1_v[:, 4 * n:4 * n + 4, bass.ds(ch * D + (b * (2 * PAIR) + q * PAIR), PAIR)])

            def ff2_loads(ch, b):
                for q in range(2):
                    for n in range(4):
                        chunk_load(ch * (2 * NPAIR) + (b * 2 + (FF_PAIR + NPAIR + q)), n,
                                   w_ff2_v[:, ch, 4 * n:4 * n + 4, bass.ds(b * (2 * PAIR) + q * PAIR, PAIR)])

            with sp.Fori(0, FC) as ch:
                with sp.Fori(0, BODIES) as b:
                    ff1_loads(ch, b)
                with sp.Fori(0, BODIES) as b:
                    ff2_loads(ch, b)
            sp.wait_ge(y_out, START + 16 * NPAIR)

        @block.gpsimd
        def _(pool):
            for started in (ada_sums, ada_added, ws_turned, z_ready, gate_ready, vg_part, scores, sgu_ready, attn_ready,
                            gated, probs_turned, x1_old, sq_added, stage_turned, h2_ready, ff_ready, y_ready, y_turned,
                            y_out, *x1_ready, *relu_ready, *ff_added):
                pool.sem_inc(started, START)
            pool.sem_inc(ada_step, ARING)
            pool.memset(ones[:, :], 1.0).then_inc(consts_made, 1)
            pool.memset(cols[:, 0:1], EPS).then_inc(consts_made, 1)
            pool.memset(cols[:, 1:2], 1.0).then_inc(consts_made, 1)
            pool.memset(mask_bf[:, :], 0.0).then_inc(consts_made, 1)
            pool.memset(neg_sel[:, :], 0.0).then_inc(consts_made, 1)
            pool.memset(rows_b[:, :], 0.0).then_inc(consts_made, 1)
            pool.wait_ge(consts_made, 6)
            pool.affine_select(out=ident[:, :], in_=ones[:, :], compare_op=ALU.is_equal, fill=0.0, base=0,
                               pattern=[[-1, P]], channel_multiplier=1).then_inc(consts_made, 1)
            pool.affine_select(out=mask01[:, :], in_=ones[:, :], compare_op=ALU.is_ge, fill=0.0, base=0,
                               pattern=[[1, P]], channel_multiplier=-1).then_inc(consts_made, 1)
            pool.affine_select(out=mask_bf[:, :], in_=mask_bf[:, :], compare_op=ALU.is_ge, fill=NEG, base=0,
                               pattern=[[-1, P]], channel_multiplier=1).then_inc(consts_made, 1)
            pool.wait_ge(consts_made, 9)
            pool.tensor_copy(ident_bf[:, :], ident[:, :]).then_inc(consts_made, 1)
            for at in (0, 32):
                pool.affine_select(out=neg_sel[:, :], in_=neg_sel[:, :], compare_op=ALU.not_equal, fill=-1.0,
                                   base=-at, pattern=[[-1, H]], channel_multiplier=1).then_inc(consts_made, 1)
                pool.wait_ge(consts_made, 11 + (at > 0))


        @block.scalar
        def _(act):
            def round_slot(pair0, j):
                n = (j % SLOTS) // 2
                act.wait_ge(raw_in[n], pair0 * 32 + 32 * (j // SLOTS + 1))
                act.wait_ge(slot_used, pair0 * SLOTS + (j + 1))
                act.activation(w_hi[:, j % SPLIT, :, :], raw[:, n, 2 * (j % 2):2 * (j % 2) + 2, :],
                               ACT.Copy).then_inc(w_rounded, 1)

            act.wait_ge(consts_made, CONSTS)
            act.wait_ge(vecs_ready, 2)
            act.activation(c_act[:, :], vec_b[:, 0:KC], ACT.Silu).then_inc(c_ready, 1)
            for i in range(ST):
                act.wait_ge(x_in[i], 16)
                act.activation(xhat[:, 4 * i:4 * i + 4, :], x_nat[:, i, :].rearrange("p (k n) -> p k n", k=4),
                               ACT.Square, accum_out=x_sum[:, i:i + 1]).then_inc(x_squared, 1)
            act.wait_ge(x_squared, ST)
            act.activation(x_root[:, :], x_sum[:, :], ACT.Sqrt, bias=cols[:, 0:1], scale=1.0 / D).then_inc(x_rooted, 1)
            act.wait_ge(x_inverted, 1)
            for i in range(ST):
                act.activation(x_nat[:, i, :], x_nat[:, i, :], ACT.Copy, scale=x_inv[:, i:i + 1]).then_inc(x_normed, 1)
            with act.Fori(0, KC // 2) as t:
                for a in range(2):
                    act.wait_ge(consts_made, CONSTS)
                    act.wait_ge(x_turned, t * 2 + (a + 1))
                    act.activation(xhat[:, bass.ds(t * 2 + a, 1), :], bank_s[:, a:a + 1, :], ACT.Copy).then_inc(xhat_ready, 1)
            act.wait_ge(small_in, 32)
            act.activation(wf[:, :, 0:H], wf_raw[:, :, :], ACT.Copy).then_inc(wf_rounded, 1)
            with act.Fori(0, GRPS) as g:
                act.wait_ge(a1_ready, g + 1)
                act.wait_ge(consts_made, CONSTS)
                for t in range(GRP):
                    n = bass.ds(g * GRP + t, 1)
                    act.activation(xhat[:, n, :], xhat[:, n, :], ACT.Identity, scale=a1[:, n], bias=mod[:, n]).then_inc(h_full, 1)
                    act.wait_ge(consts_made, CONSTS)
                    act.wait_ge(h_full, g * GRP + (t + 1))
                    act.activation(h_hi[:, n, :], xhat[:, n, :], ACT.Copy).then_inc(h_hi_ready, 1)
            for j in range(LEAD):
                round_slot(0, j)
            act.wait_ge(f_sums, GRPS)
            for i in range(ST):
                act.activation(f_two[:, i, :], f_banks[i][:, 0:2 * H], ACT.Copy).then_inc(f_copied, 1)
            act.wait_ge(f_biased, 1)
            act.activation(f_y, f_x, ACT.Abs).then_inc(f_act, 1)
            act.wait_ge(f_act, 1)
            act.activation(f_y, f_y, ACT.Exp, scale=-1.0).then_inc(f_act, 1)
            act.wait_ge(f_act, 2)
            act.activation(f_y, f_y, ACT.Ln, bias=cols[0:H, 1:2]).then_inc(f_act, 1)

            def squares_of(hp, e, bank):
                act.activation(tmp[:, e % 2, :], bank[:, e % 2, :], ACT.Square).then_inc(squares, 1)

            def roots_of(hp, e0):
                for e in (e0, e0 + 1):
                    act.wait_ge(norm_sums, hp * 4 + (e + 1))
                    src = (bank_s[:, 0, :], bank_s[:, 1, :], bank_t[:, :], bank_o[:, :])[e]
                    act.activation(tmp[:, e % 2, :], src, ACT.Sqrt, bias=cols[:, 0:1], scale=1.0 / DH).then_inc(norm_root, 1)

            def ada_loads(block, j, steps):
                for at, slot in enumerate(steps):
                    if (steps[at - ARING] + 1 if at >= ARING else 0) != j:
                        continue
                    blk, k = at // KC, at % KC
                    act.wait_ge(ada_step, (block + blk) * KC + (k + 1))
                    act.dma_start(ada_tile[:, k % ARING, :],
                                  ada_flat[k, :, bass.ds(block * AB + (GATE1 * P + blk * AB), AB)]
                                  ).then_inc(ada_in[k % ARING], 16)

            def exp_of(hp, t):
                n = P * (t % ST + 1)
                act.wait_ge(maxima, hp * 8 + (t + 1))
                act.wait_ge(probs_turned, START + hp * 8 + max(t - ST + 1, 0))
                act.activation(prob[:, t % ST, 0:n], bank_s[:, t % 2, 0:n], ACT.Exp, bias=neg_max[:, t:t + 1],
                               accum_out=row_sum[:, t:t + 1]).then_inc(exps, 1)

            def copy_prob_t(hp, t):
                i = t % ST
                act.wait_ge(probs_turned, START + hp * 8 + (t + 1))
                if t >= ST:
                    act.wait_ge(attn_sums, hp * 2 + 1)
                act.activation(prob_t[:, 0:i + 1, P * i:P * (i + 1)],
                               bank_t[:, 0:P * (i + 1)].rearrange("p (j q) -> p j q", q=P), ACT.Copy).then_inc(probs_t, 1)

            def slot_done(pair0, j):
                act.wait_ge(slot_used, pair0 * SLOTS + (j + 1 + SPLIT))

            with act.Fori(0, HP) as hp:
                pair0 = hp * STEP_PAIRS
                for j in range(STEP_SLOTS):
                    round_slot(pair0, j + LEAD)
                    ada_loads(hp * 2, j, ADA_IN)
                    if j == 7:
                        slot_done(pair0, j)
                        act.wait_ge(sgu_ready, START + hp * 2)
                        act.wait_ge(f_ready, 1)
                        for e in (0, 1):
                            squares_of(hp, e, bank_a)
                    if j == 10:
                        roots_of(hp, 0)
                    if j == 15:
                        slot_done(pair0, j)
                        act.wait_ge(qk_ready, hp * 4 + 2)
                        for e in (2, 3):
                            squares_of(hp, e, bank_b)
                    if j == 18:
                        roots_of(hp, 2)
                    if j - 1 in SCORE_AT:
                        exp_of(hp, SCORE_AT.index(j - 1))
                    if j == 23:
                        slot_done(pair0, j)
                        act.wait_ge(gated, START + hp * 2)
                        act.wait_ge(f_ready, 1)
                        for a in range(2):
                            act.activation(part[:, a, :], bank_a[:, a, :], ACT.Copy).then_inc(v_part, 1)
                    if j - 4 in SCORE_AT:
                        copy_prob_t(hp, SCORE_AT.index(j - 4))
                    if j in (25, 27):
                        a = (j - 25) // 2
                        act.wait_ge(v_turned, hp * 2 + (a + 1))
                        act.activation(v_n[:, a, :, :], bank_o[:, :].rearrange("p (i d) -> p i d", d=P),
                                       ACT.Copy).then_inc(v_ready, 1)
                    if j in (29, 35):
                        a = (j - 29) // 6
                        act.wait_ge(consts_made, CONSTS)
                        act.wait_ge(attn_sums, hp * 2 + (a + 1))
                        act.activation(mix_hi[:, bass.ds(hp * 4 + a, 1), :].rearrange("p k n -> p (k n)"),
                                       bank_o[:, :], ACT.Copy).then_inc(attn_hi, 1)
                    if j == 31:
                        slot_done(pair0, j)
                        act.wait_ge(v_turned, hp * 2 + 2)
                        for a in range(2):
                            act.activation(part[:, a, :], bank_b[:, a, :], ACT.Gelu_apprx_tanh).then_inc(vg_part, 1)
                    if j in (35, 37):
                        a = (j - 35) // 2
                        act.wait_ge(vg_agg, hp * 2 + (a + 1))
                        act.activation(vg_log[:, a, :], vg_mv[:, a, :, 1], ACT.Ln, bias=cols[:, 0:1]).then_inc(vg_logged, 1)
                        act.wait_ge(vg_logged, hp * 2 + (a + 1))
                        act.activation(vg_inv[:, a, :], vg_log[:, a, :], ACT.Exp, scale=-0.5).then_inc(vg_inverted, 1)
                    if j == 39:
                        slot_done(pair0, j)
                        for a in range(2):
                            act.activation(tmp[:, a, :], bank_s[:, a, :], ACT.Gelu_apprx_tanh).then_inc(gate_ready, 1)
                        for a in range(2):
                            act.wait_ge(consts_made, CONSTS)
                            act.wait_ge(gated, START + hp * 2 + (a + 1))
                            act.activation(mix_hi[:, bass.ds(hp * 4 + (2 + a), 1), :], tmp[:, a:a + 1, :],
                                           ACT.Copy).then_inc(sgu_hi, 1)

            with act.Fori(0, BODIES) as b:
                pair0 = b * 2 + OUT_PAIR
                for j in range(2 * SLOTS):
                    q = j // SLOTS
                    round_slot(pair0, j + LEAD)
                    ada_loads(b + OUT_BLOCK, j, ADA_BODY)
                    if j % SLOTS == 5:
                        for a in range(2):
                            act.wait_ge(consts_made, CONSTS)
                            act.wait_ge(stage_turned, START + b * 4 + (2 * q + a + 1))
                            act.activation(x1[:, bass.ds(b * 4 + (2 * q + a), 1), :], bank_s[:, a:a + 1, :],
                                           ACT.Copy).then_inc(x1_old, 1)
            act.wait_ge(sq_sums, 1)
            act.activation(inv[:, :], bank_o[:, :], ACT.Sqrt, bias=cols[:, 0:1], scale=1.0 / D).then_inc(sq_root, 1)
            with act.Fori(0, KC // 2) as t:
                for a in range(2):
                    act.wait_ge(consts_made, CONSTS)
                    act.wait_ge(h2_scaled, t * 2 + (a + 1))
                    act.activation(h_hi[:, bass.ds(t * 2 + a, 1), :], tmp[:, a:a + 1, :], ACT.Identity,
                                   bias=mod[:, bass.ds(t * 2 + (SHIFT2 + a), 1)]).then_inc(h2_hi, 1)

            def ff1_body(ch, b, ada=False):
                pair0 = ch * (2 * NPAIR) + (b * 2 + FF_PAIR)
                for j in range(2 * SLOTS):
                    round_slot(pair0, j + LEAD)
                    if ada:
                        ada_loads(b + FF_BLOCK, j, ADA_BODY)
                    if j % SLOTS == 7:
                        q = j // SLOTS
                        bank = (bank_a, bank_b)[q]
                        n0 = ch * KC + (b * 4 + 2 * q)
                        slot_done(pair0, j)
                        act.wait_ge(ff_ready, START + n0)
                        act.wait_ge(h2_ready, START + KC)
                        act.activation(tmp[:, :, :], bank[:, :, :], ACT.Relu).then_inc(relu_ready[q], 1)
                        for a in range(2):
                            act.wait_ge(consts_made, CONSTS)
                            act.wait_ge(ff_square, n0 + (a + 1))
                            act.activation(mix_hi[:, bass.ds(b * 4 + (2 * q + a), 1), :], tmp[:, a:a + 1, :],
                                           ACT.Copy).then_inc(ff_hi, 1)

            def copy_out(b, n):
                act.wait_ge(y_turned, START + n + 1)
                act.wait_ge(y_out, START + n * 16)
                act.activation(x_stage[:, :, :].rearrange("p i n -> p (i n)"),
                               bank_s[:, :, :].rearrange("p b n -> p (b n)"), ACT.Copy).then_inc(y_ready, 1)
                act.wait_ge(y_ready, START + n + 1)
                act.dma_start(out_v[:, :, bass.ds(n * PAIR, PAIR)], x_stage[:, :, :]).then_inc(y_out, 16)

            def ff2_body(ch, b, last=False, first_out=True, store=False):
                pair0 = ch * (2 * NPAIR) + (b * 2 + (FF_PAIR + NPAIR))
                for j in range(2 * SLOTS):
                    if not (last and j + LEAD >= 2 * SLOTS):
                        round_slot(pair0, j + LEAD)
                    if store and j == 3 and not first_out:
                        copy_out(b, b * 2 - 1)
                    if store and j == 11:
                        copy_out(b, b * 2)

            with act.Fori(0, BODIES) as b:
                ff1_body(0, b, ada=True)
            with act.Fori(0, FC - 1) as ch:
                with act.Fori(0, BODIES) as b:
                    ff2_body(ch, b)
                with act.Fori(0, BODIES) as b:
                    ff1_body(ch + 1, b)
            ff2_body(FC - 1, 0, store=True)
            with act.Fori(1, BODIES - 1) as b:
                ff2_body(FC - 1, b, first_out=False, store=True)
            ff2_body(FC - 1, BODIES - 1, last=True, first_out=False, store=True)
            copy_out(BODIES, NPAIR - 1)

        @block.vector
        def _(dve):
            def split_slot(pair0, j):
                n = (j % SLOTS) // 2
                dve.wait_ge(w_rounded, pair0 * SLOTS + (j + 1))
                dve.tensor_tensor(w_lo[:, j % SPLIT, :, :], raw[:, n, 2 * (j % 2):2 * (j % 2) + 2, :],
                                  w_hi[:, j % SPLIT, :, :].bitcast(F32), ALU.subtract).then_inc(w_split, 1)

            dve.memset(f_split[:, :].bitcast(F32), 0.0).then_inc(w_split, 2 * RAW)
            dve.memset(f_ones, 1.0).then_inc(f_cleared, 1)
            dve.wait_ge(rows_turned, 1)
            dve.tensor_copy(vec_b[:, :], bank_o[:, P:2 * P]).then_inc(vecs_ready, 1)
            dve.tensor_copy(vec_a[:, :], bank_o[:, 0:P]).then_inc(vecs_ready, 1)
            dve.wait_ge(vecs_ready, 2)
            dve.tensor_scalar(gq_scaled[:, :], vec_b[:, KC + G:KC + G + 1], float(DH) ** -0.5, None,
                              ALU.mult).then_inc(gq_ready, 1)
            dve.wait_ge(x_rooted, 1)
            dve.reciprocal(x_inv[:, :], x_root[:, :]).then_inc(x_inverted, 1)
            dve.wait_ge(c_ready, 1)

            dve.wait_ge(wf_rounded, 1)
            dve.tensor_tensor(wf[:, :, H:2 * H], wf_raw[:, :, :], wf[:, :, 0:H].bitcast(F32), ALU.subtract).then_inc(wf_ready, 1)

            def mod_group_step(g, k):
                dve.wait_ge(mod_in[k % MRING], g * (16 * KC // MRING) + 16 * (k // MRING + 1))
                if k == 0:
                    dve.wait_ge(mod_sums, g)
                    dve.tensor_scalar(mod_acc[:, :, :], mod_tile[:, k % MRING, :, :], c_act[:, k:k + 1], None,
                                      ALU.mult).then_inc(mod_step, 1)
                else:
                    dve.wait_ge(mod_step, g * KC + k)
                    dve.scalar_tensor_tensor(out=mod_acc[:, :, :], in0=mod_tile[:, k % MRING, :, :], scalar=c_act[:, k:k + 1],
                                             in1=mod_acc[:, :, :], op0=ALU.mult, op1=ALU.add).then_inc(mod_step, 1)

            def mod_group_add(g):
                dve.wait_ge(mod_sums, g + 1)
                for m in range(2):
                    at = bass.ds(g * GRP + m * KC, GRP)
                    dve.tensor_tensor(mod[:, at], bank_t[:, m * GRP:(m + 1) * GRP], vec_a[:, at],
                                      ALU.add).then_inc(mod_added, 1)
                dve.wait_ge(mod_added, g * 2 + 2)
                dve.scalar_tensor_tensor(out=a1[:, bass.ds(g * GRP, GRP)], in0=mod[:, bass.ds(g * GRP + SCALE1, GRP)],
                                         scalar=1.0, in1=vec_a[:, bass.ds(g * GRP + 6 * KC, GRP)],
                                         op0=ALU.add, op1=ALU.mult).then_inc(a1_ready, 1)

            def h_low(g, t):
                n = bass.ds(g * GRP + t, 1)
                dve.wait_ge(h_hi_ready, g * GRP + (t + 1))
                dve.tensor_tensor(h_lo[:, n, :], xhat[:, n, :], h_hi[:, n, :].bitcast(F32), ALU.subtract).then_inc(h_ready, 1)

            for k in range(KC):
                mod_group_step(0, k)
            with dve.Fori(1, GRPS) as g:
                for k in range(KC):
                    mod_group_step(g, k)
                    if k == 1:
                        mod_group_add(g - 1)
                    if k in (4, 6, 8, 10):
                        h_low(g - 1, (k - 4) // 2)
            mod_group_add(GRPS - 1)
            for t in range(GRP):
                h_low(GRPS - 1, t)
            for j in range(LEAD):
                split_slot(0, j)
            dve.wait_ge(f_copied, ST)
            dve.tensor_tensor(f_nat[:, :, :], f_two[:, :, 0:H], f_two[:, :, H:2 * H], ALU.add).then_inc(f_joined, 1)
            dve.wait_ge(f_turned, 1)
            dve.tensor_scalar(f_x, bank_o[0:H, :], bf_col[:, 0:1], None, ALU.add).then_inc(f_biased, 1)
            dve.wait_ge(f_act, 3)
            dve.scalar_tensor_tensor(out=f_x, in0=f_x, scalar=0.0, in1=f_y, op0=ALU.min, op1=ALU.subtract).then_inc(f_log, 1)
            dve.wait_ge(f_log, 1)
            dve.tensor_tensor_scan(f_cum, f_ones, f_x, 0.0, ALU.mult, ALU.add).then_inc(f_summed, 1)
            dve.wait_ge(f_summed, 1)
            dve.tensor_copy(f_split[0:H, :], f_cum).then_inc(f_hi_ready, 1)
            dve.wait_ge(f_hi_ready, 1)
            dve.tensor_tensor(f_split[32:32 + H, :], f_cum, f_split[0:H, :].bitcast(F32), ALU.subtract).then_inc(f_ready, 1)

            def norm_of(hp, e, bank):
                a = e % 2
                dve.wait_ge(norm_root, hp * 4 + (e + 1))
                dve.reciprocal(tmp[:, a, :], tmp[:, a, :]).then_inc(norm_inv, 1)
                dve.wait_ge(norm_inv, hp * 4 + (e + 1))
                dst, g = ((q_t, gq_scaled[:, 0:1]), (k_t, vec_b[:, KC + G + 1:KC + G + 2]))[e // 2]
                dve.scalar_tensor_tensor(out=dst[:, a, :], in0=bank[:, a, :], scalar=g, in1=tmp[:, a, :],
                                         op0=ALU.mult, op1=ALU.mult).then_inc(qk_ready, 1)

            def ada_steps(block, j, steps):
                for at, slot in enumerate(steps):
                    if slot != j:
                        continue
                    blk, k = at // KC, at % KC
                    dve.wait_ge(ada_in[k % ARING], block * (16 * KC // ARING) + (blk * (16 * KC // ARING) + 16 * (k // ARING + 1)))
                    if k == 0:
                        dve.wait_ge(ada_sums, START + block + blk)
                        dve.tensor_scalar(ada_acc[:, :], ada_tile[:, k % ARING, :], c_act[:, k:k + 1], None,
                                          ALU.mult).then_inc(ada_step, 1)
                    else:
                        dve.wait_ge(ada_step, ARING + block * KC + (blk * KC + k))
                        dve.scalar_tensor_tensor(out=ada_acc[:, :], in0=ada_tile[:, k % ARING, :], scalar=c_act[:, k:k + 1],
                                                 in1=ada_acc[:, :], op0=ALU.mult, op1=ALU.add).then_inc(ada_step, 1)

            def ada_add(block, src):
                dve.wait_ge(ada_sums, START + block + 1)
                at = bass.ds(block * ABT + GATE1, ABT)
                dve.tensor_tensor(mod[:, at], src[:, 0:ABT], vec_a[:, at], ALU.add).then_inc(ada_added, 1)

            def max_of(hp, t):
                dve.wait_ge(scores, START + hp * 8 + (t + 1))
                dve.reduce_max(neg_max[:, t:t + 1], bank_s[:, t % 2, 0:P * (t % ST + 1)], AX_X,
                               negate=True).then_inc(maxima, 1)

            def scale_of(hp, t):
                n = P * (t % ST + 1)
                dve.wait_ge(exps, hp * 8 + (t + 1))
                dve.reciprocal(row_inv[:, t:t + 1], row_sum[:, t:t + 1]).then_inc(sums_inv, 1)
                dve.wait_ge(sums_inv, hp * 8 + (t + 1))
                dve.tensor_scalar(prob[:, t % ST, 0:n], prob[:, t % ST, 0:n], row_inv[:, t:t + 1], None,
                                  ALU.mult).then_inc(probs, 1)

            def vg_norm_stats(hp, a):
                src = (bank_t, bank_o)[a]
                dve.wait_ge(vg_turned, hp * 2 + (a + 1))
                for i in range(ST):
                    dve.bn_stats(vg_stats[:, a, i, :], src[:, P * i:P * (i + 1)]).then_inc(vg_stat, 1)
                dve.wait_ge(consts_made, CONSTS)
                dve.wait_ge(vg_stat, hp * (2 * ST) + ST * (a + 1))
                for i in range(ST):
                    ins = dve.bn_aggr(vg_mv[:, a, i, :], vg_stats[:, a, i, :])
                ins.then_inc(vg_agg, 1)

            def vg_norm(hp, a):
                src = (bank_t, bank_o)[a]
                dve.wait_ge(vg_inverted, hp * 2 + (a + 1))
                for i in range(ST):
                    ins = dve.tensor_scalar(vg_n[:, a, i, :], src[:, P * i:P * (i + 1)], vg_mv[:, a, i, 0:1],
                                            vg_inv[:, a, i:i + 1], ALU.subtract, ALU.mult)
                ins.then_inc(vg_ready, 1)

            with dve.Fori(0, HP) as hp:
                pair0 = hp * STEP_PAIRS
                for j in range(STEP_SLOTS):
                    split_slot(pair0, j + LEAD)
                    ada_steps(hp * 2, j, ADA_IN)
                    if j == 0:
                        dve.wait_ge(consts_made, CONSTS)
                        dve.wait_ge(scores, START + hp * 8)
                        dve.tensor_copy(sel_cur[:, :, :], neg_sel[:, bass.ds(hp * 2, 2)].unsqueeze(2).to_broadcast([P, 2, P])
                                        ).then_inc(sel_ready, 1)
                    if j == 4:
                        dve.wait_ge(ws_turned, START + hp + 1)
                        for a in range(2):
                            dve.tensor_tensor(ws_t[:, a, :], bank_t[:, P * a:P * (a + 1)], mask01[:, :], ALU.mult).then_inc(ws_ready, 1)
                    if j in (10, 12):
                        norm_of(hp, (j - 10) // 2, bank_a)
                    if j in (18, 20):
                        norm_of(hp, 2 + (j - 18) // 2, bank_b)
                    if j == 21:
                        ada_add(hp * 2, bank_t)
                    if j - 1 in SCORE_AT:
                        max_of(hp, SCORE_AT.index(j - 1))
                    if j - 2 in SCORE_AT:
                        scale_of(hp, SCORE_AT.index(j - 2))
                    if j in (29, 35):
                        a = (j - 29) // 6
                        dve.wait_ge(attn_hi, hp * 2 + (a + 1))
                        m = bass.ds(hp * 4 + a, 1)
                        dve.tensor_tensor(mix_lo[:, m, :].rearrange("p k n -> p (k n)"), bank_o[:, :],
                                          mix_hi[:, m, :].rearrange("p k n -> p (k n)").bitcast(F32),
                                          ALU.subtract).then_inc(attn_ready, 1)
                    if j in (35, 37):
                        vg_norm_stats(hp, (j - 35) // 2)
                    if j in (36, 38):
                        vg_norm(hp, (j - 36) // 2)
                    if j == 39:
                        dve.wait_ge(bs_in, hp * 16 + 16)
                        for a in range(2):
                            dve.wait_ge(z_sums, hp * 2 + (a + 1))
                            dve.scalar_tensor_tensor(out=part[:, a, :].rearrange("p (i t) -> p i t", t=P),
                                                     in0=(bank_t, bank_o)[a][:, :].rearrange("p (i t) -> p i t", t=P),
                                                     scalar=vec_b[:, bass.ds(hp * 2 + (KC + a), 1)],
                                                     in1=bs_all[:, a:a + 1, :].to_broadcast([P, ST, P]),
                                                     op0=ALU.mult, op1=ALU.add).then_inc(z_ready, 1)
                    if j == 39:
                        dve.wait_ge(z_ready, START + hp * 2 + 2)
                        for a in range(2):
                            dve.wait_ge(gate_ready, START + hp * 2 + (a + 1))
                            dve.tensor_tensor(tmp[:, a, :], tmp[:, a, :], part[:, a, :], ALU.mult).then_inc(gated, 1)
                        for a in range(2):
                            m = bass.ds(hp * 4 + (2 + a), 1)
                            dve.wait_ge(sgu_hi, hp * 2 + (a + 1))
                            dve.tensor_tensor(mix_lo[:, m, :], tmp[:, a:a + 1, :], mix_hi[:, m, :].bitcast(F32),
                                              ALU.subtract).then_inc(sgu_ready, 1)
                        ada_add(hp * 2 + 1, bank_a[:, 0, :])

            dve.wait_ge(gated, START + 2 * HP)
            dve.memset(sq_acc[:, :], 0.0).then_inc(sq_cleared, 1)
            with dve.Fori(0, BODIES) as b:
                pair0 = b * 2 + OUT_PAIR
                for j in range(2 * SLOTS):
                    split_slot(pair0, j + LEAD)
                    ada_steps(b + OUT_BLOCK, j, ADA_BODY)
                    if j % SLOTS == 7:
                        q = j // SLOTS
                        bank = (bank_a, bank_b)[q]
                        dve.wait_ge(slot_used, pair0 * SLOTS + (j + 1 + SPLIT))
                        dve.wait_ge(ada_added, START + OUT_BLOCK)
                        for a in range(2):
                            n = bass.ds(b * 4 + (2 * q + a), 1)
                            dve.wait_ge(x1_old, START + b * 4 + (2 * q + a + 1))
                            dve.scalar_tensor_tensor(out=x1[:, n, :], in0=bank[:, a:a + 1, :],
                                                     scalar=mod[:, bass.ds(b * 4 + (GATE1 + 2 * q + a), 1)],
                                                     in1=x1[:, n, :], op0=ALU.mult, op1=ALU.add).then_inc(x1_ready[q], 1)
                        for a in range(2):
                            n = bass.ds(b * 4 + (2 * q + a), 1)
                            dve.wait_ge(x1_ready[q], START + b * 2 + (a + 1))
                            dve.tensor_tensor(tmp[:, a:a + 1, :], x1[:, n, :], x1[:, n, :], ALU.mult).then_inc(x1_square, 1)
                            dve.wait_ge(x1_square, b * 4 + (2 * q + a + 1))
                            dve.wait_ge(sq_added, START + b * 4 + (2 * q + a))
                            dve.wait_ge(sq_cleared, 1)
                            dve.tensor_tensor(sq_acc[:, :], sq_acc[:, :], tmp[:, a, :], ALU.add).then_inc(sq_added, 1)
                    if j == 15:
                        ada_add(b + OUT_BLOCK, bank_t)
            dve.wait_ge(ada_added, START + FF_BLOCK)
            dve.scalar_tensor_tensor(out=a2[:, :], in0=mod[:, SCALE2:SCALE2 + KC], scalar=1.0,
                                     in1=vec_a[:, 7 * KC:8 * KC], op0=ALU.add, op1=ALU.mult).then_inc(a2_ready, 1)
            dve.wait_ge(sq_root, 1)
            dve.reciprocal(inv[:, :], inv[:, :]).then_inc(inv_ready, 1)
            dve.wait_ge(inv_ready, 1)
            dve.wait_ge(a2_ready, 1)
            with dve.Fori(0, KC // 2) as t:
                for a in range(2):
                    dve.wait_ge(h2_ready, START + t * 2)
                    dve.scalar_tensor_tensor(out=tmp[:, a, :], in0=x1[:, bass.ds(t * 2 + a, 1), :].rearrange("p k n -> p (k n)"),
                                             scalar=a2[:, bass.ds(t * 2 + a, 1)], in1=inv[:, :],
                                             op0=ALU.mult, op1=ALU.mult).then_inc(h2_scaled, 1)
                for a in range(2):
                    n = bass.ds(t * 2 + a, 1)
                    dve.wait_ge(h2_hi, t * 2 + (a + 1))
                    dve.scalar_tensor_tensor(out=h_lo[:, n, :], in0=tmp[:, a:a + 1, :],
                                             scalar=mod[:, bass.ds(t * 2 + (SHIFT2 + a), 1)],
                                             in1=h_hi[:, n, :].bitcast(F32), op0=ALU.add, op1=ALU.subtract).then_inc(h2_ready, 1)

            def ff1_body(ch, b, ada=False):
                pair0 = ch * (2 * NPAIR) + (b * 2 + FF_PAIR)
                for j in range(2 * SLOTS):
                    split_slot(pair0, j + LEAD)
                    if ada:
                        ada_steps(b + FF_BLOCK, j, ADA_BODY)
                        if j == 15:
                            ada_add(b + FF_BLOCK, bank_t)
                    if j % SLOTS == 7:
                        q = j // SLOTS
                        n0 = ch * KC + (b * 4 + 2 * q)
                        dve.wait_ge(relu_ready[q], START + ch * BODIES + (b + 1))
                        for a in range(2):
                            dve.tensor_tensor(tmp[:, a, :], tmp[:, a, :], tmp[:, a, :], ALU.mult).then_inc(ff_square, 1)
                        for a in range(2):
                            m = bass.ds(b * 4 + (2 * q + a), 1)
                            dve.wait_ge(ff_hi, n0 + (a + 1))
                            dve.tensor_tensor(mix_lo[:, m, :], tmp[:, a:a + 1, :], mix_hi[:, m, :].bitcast(F32),
                                              ALU.subtract).then_inc(ff_ready, 1)

            def ff2_body(ch, b, last=False, final=False):
                pair0 = ch * (2 * NPAIR) + (b * 2 + (FF_PAIR + NPAIR))
                for j in range(2 * SLOTS):
                    if not (last and j + LEAD >= 2 * SLOTS):
                        split_slot(pair0, j + LEAD)
                    if j % SLOTS == 7:
                        q = j // SLOTS
                        bank = (bank_a, bank_b)[q]
                        dve.wait_ge(slot_used, pair0 * SLOTS + (j + 1 + SPLIT))
                        dve.wait_ge(ada_added, START + FF_BLOCK + BODIES)
                        if final:
                            dve.wait_ge(y_turned, START + b * 2 + q)
                        for a in range(2):
                            n = bass.ds(b * 4 + (2 * q + a), 1)
                            dve.scalar_tensor_tensor(out=part[:, a:a + 1, :] if final else x1[:, n, :],
                                                     in0=bank[:, a:a + 1, :],
                                                     scalar=mod[:, bass.ds(b * 4 + (GATE2 + 2 * q + a), 1)],
                                                     in1=x1[:, n, :], op0=ALU.mult, op1=ALU.add).then_inc(ff_added[q], 1)

            with dve.Fori(0, BODIES) as b:
                ff1_body(0, b, ada=True)
            with dve.Fori(0, FC - 1) as ch:
                with dve.Fori(0, BODIES) as b:
                    ff2_body(ch, b)
                with dve.Fori(0, BODIES) as b:
                    ff1_body(ch + 1, b)
            with dve.Fori(0, BODIES - 1) as b:
                ff2_body(FC - 1, b, final=True)
            ff2_body(FC - 1, BODIES - 1, last=True, final=True)

        @block.tensor
        def _(pe):
            def product(dst, w_slot, kk, a, act_k, hi, lo, first, last):
                wh = w_hi[:, w_slot, kk, P * a:P * (a + 1)]
                wl = w_lo[:, w_slot, kk, P * a:P * (a + 1)]
                pe.matmul(dst, lhsT=wh, rhs=hi[:, act_k, :], start=first, stop=False)
                pe.matmul(dst, lhsT=wh, rhs=lo[:, act_k, :], start=False, stop=False)
                return pe.matmul(dst, lhsT=wl, rhs=hi[:, act_k, :], start=False, stop=last)

            def slot(pair0, j, bank, hi, lo):
                pe.wait_ge(w_split, pair0 * SLOTS + (j + 1 + 2 * RAW))
                for kk in range(2):
                    k = 2 * (j % SLOTS) + kk
                    for a in range(2):
                        ins = product(bank[:, a, :], j % SPLIT, kk, a, k, hi, lo, k == 0, k == KC - 1)
                ins.then_inc(slot_used, 1)

            pe.wait_ge(consts_made, CONSTS)
            pe.wait_ge(rows_in, 16 * 7)
            pe.transpose(bank_o[:, P:2 * P], rows_b[:, :], ident[:, :]).then_inc(slot_used, SPLIT)
            pe.transpose(bank_o[:, 0:P], rows_a[:, :], ident[:, :]).then_inc(rows_turned, 1)
            pe.wait_ge(x_normed, ST)
            for t in range(KC):
                if t >= 2:
                    pe.wait_ge(xhat_ready, t - 1)
                for i in range(ST):
                    ins = pe.transpose(bank_s[:, t % 2, P * i:P * (i + 1)], x_nat[:, i, P * t:P * (t + 1)], ident[:, :])
                ins.then_inc(x_turned, 1)

            def column_sums(acc, n, dst):
                for t in range(n):
                    ins = pe.matmul(dst[:, t:t + 1], lhsT=acc[:, P * t:P * (t + 1)], rhs=ones[:, 0:1], start=True, stop=True)
                return ins

            def f_logits(g):
                pe.wait_ge(wf_ready, 1)
                pe.wait_ge(vecs_ready, 2)
                pe.wait_ge(xhat_ready, KC)
                pe.wait_ge(h_ready, (g + 1) * GRP)
                for k in range(g * GRP, (g + 1) * GRP):
                    for act_h in (h_hi, h_lo):
                        for i in range(ST):
                            ins = pe.matmul(f_banks[i][:, 0:2 * H], lhsT=act_h[:, k, P * i:P * (i + 1)], rhs=wf[:, k, :],
                                            start=(k == 0 and act_h is h_hi), stop=(k == KC - 1 and act_h is h_lo))
                ins.then_inc(f_sums, 1)

            for g in range(GRPS):
                if g >= 1:
                    f_logits(g - 1)
                    pe.wait_ge(mod_added, 2 * g)
                pe.wait_ge(mod_step, (g + 1) * KC)
                for m in range(2):
                    ins = column_sums(mod_acc[:, m, :], GRP, bank_t[:, m * GRP:(m + 1) * GRP])
                ins.then_inc(mod_sums, 1)
            f_logits(GRPS - 1)

            pe.wait_ge(f_joined, 1)
            for i in range(ST):
                ins = pe.matmul(bank_o[0:H, P * i:P * (i + 1)], lhsT=f_nat[:, i, :], rhs=ident[:, :], start=True, stop=True)
            ins.then_inc(f_turned, 1)

            def head_slot_tasks(hp, j):
                if j == 3:
                    pe.wait_ge(ws_in, hp * 16 + 16)
                    pe.wait_ge(z_ready, START + hp * 2)
                    for a in range(2):
                        ins = pe.transpose(bank_t[:, P * a:P * (a + 1)], ws_nat[:, a, :], ident[:, :])
                    ins.then_inc(ws_turned, 1)
                if j in (9, 17):
                    for a in range(2):
                        e = 2 * (j // SLOTS - 1) + a
                        pe.wait_ge(squares, hp * 4 + (e + 1))
                        if e == 0:
                            pe.wait_ge(gate_ready, START + hp * 2)
                        if e == 2:
                            pe.wait_ge(ws_ready, hp * 2 + 2)
                        if e == 3:
                            pe.wait_ge(z_ready, START + hp * 2)
                            pe.wait_ge(f_biased, 1)
                        dst = (bank_s[:, 0, :], bank_s[:, 1, :], bank_t[:, :], bank_o[:, :])[e]
                        pe.matmul(dst, lhsT=ones[:, :], rhs=tmp[:, a, :], start=True, stop=True).then_inc(norm_sums, 1)
                if j == 20:
                    pe.wait_ge(norm_root, hp * 4 + 3)
                    pe.wait_ge(ada_step, ARING + hp * (2 * KC) + KC)
                    column_sums(ada_acc, ABT, bank_t).then_inc(ada_sums, 1)
                if j in SCORE_AT:
                    t = SCORE_AT.index(j)
                    a, i = t // ST, t % ST
                    n = P * (i + 1)
                    dst = bank_s[:, t % 2, :]
                    pe.wait_ge(qk_ready, hp * 4 + (3 + a))
                    if t < 2:
                        pe.wait_ge(norm_root, hp * 4 + 2)
                    else:
                        pe.wait_ge(exps, hp * 8 + (t - 1))
                    if t == 0:
                        pe.wait_ge(sel_ready, hp + 1)
                        pe.wait_ge(f_ready, 1)
                    pe.matmul(dst[:, 0:n], lhsT=q_t[:, a, P * i:P * (i + 1)], rhs=k_t[:, a, 0:n], start=True, stop=False)
                    pe.matmul(dst[:, 0:n], lhsT=sel_cur[:, a, :], rhs=f_split[:, 0:n], start=False, stop=False)
                    pe.matmul(dst[:, P * i:n], lhsT=ident_bf[:, :], rhs=mask_bf[:, :], start=False, stop=True).then_inc(scores, 1)
                if j in (24, 26):
                    a = (j - 24) // 2
                    pe.wait_ge(v_part, hp * 2 + (a + 1))
                    if a == 0:
                        pe.wait_ge(norm_root, hp * 4 + 4)
                    else:
                        pe.wait_ge(v_ready, hp * 2 + 1)
                    for i in range(ST):
                        ins = pe.transpose(bank_o[:, P * i:P * (i + 1)], part[:, a, P * i:P * (i + 1)], ident[:, :])
                    ins.then_inc(v_turned, 1)
                if j - 3 in SCORE_AT:
                    t = SCORE_AT.index(j - 3)
                    i = t % ST
                    pe.wait_ge(probs, hp * 8 + (t + 1))
                    if t == 0:
                        pe.wait_ge(ada_added, START + hp * 2 + 1)
                    else:
                        pe.wait_ge(probs_t, hp * 8 + t)
                    for jj in range(i + 1):
                        ins = pe.transpose(bank_t[:, P * jj:P * (jj + 1)], prob[:, i, P * jj:P * (jj + 1)], ident[:, :])
                    ins.then_inc(probs_turned, 1)
                if j in (28, 34):
                    a = (j - 28) // 6
                    pe.wait_ge(probs_t, hp * 8 + ST * (a + 1))
                    if a == 0:
                        pe.wait_ge(v_ready, hp * 2 + 2)
                    else:
                        pe.wait_ge(attn_ready, START + hp * 2 + 1)
                    for i in range(ST):
                        ins = pe.matmul(bank_o[:, P * i:S], lhsT=v_n[:, a, i, :], rhs=prob_t[:, i, P * i:S],
                                        start=(i == 0), stop=(i == ST - 1))
                    ins.then_inc(attn_sums, 1)
                if j in (35, 36):
                    a = j - 35
                    dst = (bank_t, bank_o)[a]
                    pe.wait_ge(vg_part, START + hp * 2 + (a + 1))
                    if a == 0:
                        pe.wait_ge(probs_t, hp * 8 + 8)
                    else:
                        pe.wait_ge(attn_ready, START + hp * 2 + 2)
                    for i in range(ST):
                        ins = pe.transpose(dst[:, P * i:P * (i + 1)], part[:, a, P * i:P * (i + 1)], ident[:, :])
                    ins.then_inc(vg_turned, 1)
                if j == 38:
                    pe.wait_ge(v_part, hp * 2 + 2)
                    pe.wait_ge(ada_step, ARING + hp * (2 * KC) + 2 * KC)
                    column_sums(ada_acc, ABT, bank_a[:, 0, :]).then_inc(ada_sums, 1)
                if j in (38, 39):
                    a = j - 38
                    dst = (bank_t, bank_o)[a]
                    pe.wait_ge(vg_ready, hp * 2 + (a + 1))
                    pe.wait_ge(ws_ready, hp * 2 + 2)
                    for i in range(ST):
                        ins = pe.matmul(dst[:, P * i:P * (i + 1)], lhsT=vg_n[:, a, i, :], rhs=ws_t[:, a, :],
                                        start=True, stop=True)
                    ins.then_inc(z_sums, 1)

            with pe.Fori(0, HP) as hp:
                for j in range(STEP_SLOTS):
                    if j == 0:
                        pe.wait_ge(ada_added, START + hp * 2)
                    if j == SLOTS:
                        pe.wait_ge(vg_part, START + hp * 2)
                    if j == 2 * SLOTS:
                        pe.wait_ge(qk_ready, hp * 4 + 2)
                    if j == 3 * SLOTS:
                        pe.wait_ge(qk_ready, hp * 4 + 4)
                    if j == 4 * SLOTS:
                        pe.wait_ge(exps, hp * 8 + 8)
                    slot(hp * STEP_PAIRS, j, (bank_a, bank_b, bank_a, bank_b, bank_s)[j // SLOTS], h_hi, h_lo)
                    head_slot_tasks(hp, j)

            def block_sums(block):
                pe.wait_ge(z_ready, START + HP * 2)
                pe.wait_ge(ada_added, START + block)
                pe.wait_ge(ada_step, ARING + block * KC + KC)
                column_sums(ada_acc, ABT, bank_t).then_inc(ada_sums, 1)

            with pe.Fori(0, BODIES) as b:
                for j in range(2 * SLOTS):
                    q = j // SLOTS
                    if j % SLOTS == 0:
                        pe.wait_ge((ada_added, vg_part)[q], START + HP * 2)
                        pe.wait_ge(x1_ready[q], START + b * 2)
                    if q == 0:
                        pe.wait_ge((attn_ready, sgu_ready)[j % 2], START + 2 * (j // 2 + 1))
                    slot(b * 2 + OUT_PAIR, j, (bank_a, bank_b)[q], mix_hi, mix_lo)
                    if j % SLOTS == 3:
                        pe.wait_ge(stage_in, b * 32 + 16 * (q + 1))
                        pe.wait_ge(gate_ready, START + HP * 2)
                        pe.wait_ge(x1_old, START + b * 4 + 2 * q)
                        for a in range(2):
                            for i in range(ST):
                                ins = pe.transpose(bank_s[:, a, P * i:P * (i + 1)], x_stage[:, i, P * a:P * (a + 1)], ident[:, :])
                            ins.then_inc(stage_turned, 1)
                    if j == 14:
                        block_sums(b + OUT_BLOCK)
            pe.wait_ge(sq_added, START + KC)
            pe.wait_ge(z_ready, START + HP * 2)
            pe.matmul(bank_o[:, :], lhsT=ones[:, :], rhs=sq_acc[:, :], start=True, stop=True).then_inc(sq_sums, 1)

            def ff1_body(ch, b, ada=False):
                for j in range(2 * SLOTS):
                    q = j // SLOTS
                    if j % SLOTS == 0:
                        pe.wait_ge(x1_ready[q], START + 2 * BODIES)
                        pe.wait_ge(relu_ready[q], START + ch * BODIES + b)
                        pe.wait_ge(ff_added[q], START + ch * (2 * BODIES))
                    if q == 0:
                        pe.wait_ge(h2_ready, START + 2 * j + 2)
                    slot(ch * (2 * NPAIR) + (b * 2 + FF_PAIR), j, (bank_a, bank_b)[q], h_hi, h_lo)
                    if ada and j == 14:
                        block_sums(b + FF_BLOCK)

            def turn_out(b, n):
                q = 1 if n is None else 0
                pair = b * 2 + q
                pe.wait_ge(ff_added[q], START + (FC - 1) * 2 * BODIES + (b * 2 + 2))
                pe.wait_ge(y_ready, START + pair)
                flat = bank_s[:, :, :].rearrange("p b n -> p (b n)")
                for i in range(ST):
                    for a in range(2):
                        at = PAIR * i + P * a
                        ins = pe.transpose(flat[:, at:at + P], part[:, a, P * i:P * (i + 1)], ident[:, :])
                ins.then_inc(y_turned, 1)

            def ff2_body(ch, b, final=False, first=False):
                for j in range(2 * SLOTS):
                    q = j // SLOTS
                    if j % SLOTS == 0:
                        pe.wait_ge(relu_ready[q], START + ch * BODIES + BODIES)
                        pe.wait_ge(ff_added[q], START + ch * (2 * BODIES) + b * 2)
                    if q == 0:
                        pe.wait_ge(ff_ready, START + ch * KC + (2 * j + 2))
                    slot(ch * (2 * NPAIR) + (b * 2 + (FF_PAIR + NPAIR)), j, (bank_a, bank_b)[q], mix_hi, mix_lo)
                    if final and not first and j == 2:
                        turn_out(b - 1, None)
                    if final and j == 10:
                        turn_out(b, 0)

            with pe.Fori(0, BODIES) as b:
                ff1_body(0, b, ada=True)
            with pe.Fori(0, FC - 1) as ch:
                with pe.Fori(0, BODIES) as b:
                    ff2_body(ch, b)
                with pe.Fori(0, BODIES) as b:
                    ff1_body(ch + 1, b)
            ff2_body(FC - 1, 0, final=True, first=True)
            with pe.Fori(1, BODIES) as b:
                ff2_body(FC - 1, b, final=True)
            turn_out(BODIES - 1, None)


_INS = ["x", "c", "w_ada", "b_ada", "g_mix", "w_in", "b_f", "g_q", "g_k", "g_sgu", "w_s", "b_s",
        "w_out", "g_ffn", "w_ff1", "w_ff2"]


def kernel(**inputs):
    import numpy as np
    import concourse.bacc as bacc
    from concourse.bass_utils import run_bass_kernel_spmd

    nc = bacc.Bacc("TRN2", target_bir_lowering=False, num_devices=1, dynamic_dma_scratch_size=1024)
    arrays, args = {}, []
    for name in _INS:
        a = np.ascontiguousarray(inputs[name])
        arrays[f"in_{name}"] = a
        args.append(nc.dram_tensor(f"in_{name}", a.shape, mybir.dt.from_np(a.dtype), kind="ExternalInput").ap())
    shape = arrays["in_x"].shape
    out = nc.dram_tensor("out_0", shape, F32, kind="ExternalOutput").ap()
    block_program(nc, *args, out)
    r = run_bass_kernel_spmd(nc, [arrays], core_ids=[0])
    return r.results[0]["out_0"]
```

```python
from contextlib import ExitStack

import concourse.bass as bass
from concourse import mybir

P = 128
F32 = mybir.dt.float32
F32R = mybir.dt.float32r
BF16 = mybir.dt.bfloat16
ALU = mybir.AluOpType
ACT = mybir.ActivationFunctionType
AX_X = mybir.AxisListType.X
EPS = 1e-6
NEG = -1.0e30


def block_program(nc, x, c, w_ada, b_ada, g_mix, w_in, b_f, g_q, g_k, g_sgu, w_s, b_s,
                  w_out, g_ffn, w_ff1, w_ff2, out):
    _, S, D = x.shape
    H = b_f.shape[1]
    G = g_sgu.shape[1]
    DH = g_q.shape[1]
    AW = H * DH
    GW = G * P
    DFF = w_ff1.shape[2]
    KC = D // P
    ST = S // P
    HP = H // 2
    FC = DFF // D
    PAIR = 2 * P
    SLOTS = KC // 2
    NPAIR = D // PAIR
    BODIES = NPAIR // 2
    LEAD = 3
    STEP_PAIRS = 5
    STEP_SLOTS = STEP_PAIRS * SLOTS
    OUT_PAIR = HP * STEP_PAIRS
    FF_PAIR = OUT_PAIR + NPAIR
    CONSTS = 12
    START = 1
    RAW = 4
    SPLIT = 4
    assert (S, KC, ST, DH, H, G, AW, GW) == (512, 16, 4, P, G, H, GW, AW) and FC == 4

    COL_K, COL_V, COL_F = AW, 2 * AW, 3 * AW
    COL_U = COL_F + H
    COL_VG = COL_U + GW
    SHIFT1, SCALE1, GATE1, SHIFT2, SCALE2, GATE2 = (n * KC for n in range(6))

    GRP = 4
    GRPS = KC // GRP
    GC = GRP * P
    MRING = 8
    ABT = 4
    AB = ABT * P
    ARING = 4
    OUT_BLOCK = 2 * HP
    FF_BLOCK = OUT_BLOCK + BODIES
    ADA_IN = [2, 3, 4, 5, 6, 7, 8, 9, 11, 13, 14, 15, 16, 17, 17, 19,
              22, 23, 24, 25, 26, 27, 28, 29, 30, 30, 31, 32, 33, 34, 35, 36]
    ADA_FIRST = [6, 7, 7, 8, 8, 9, 9, 10, 10, 11, 11, 12, 12, 13, 13, 14]
    ADA_BODY = [2, 3, 4, 5, 6, 8, 8, 9, 9, 10, 10, 11, 12, 12, 13, 13]
    SCORE_AT = [21, 22, 23, 24, 26, 27, 28, 29]
    assert len(ADA_IN) == 2 * KC and len(ADA_BODY) == KC == len(ADA_FIRST) and FF_BLOCK * ABT == GATE2 - GATE1

    with ExitStack() as ctx:
        def sb(name, shape, dt=F32, where=ctx):
            return where.enter_context(nc.sbuf_tensor(name, shape, dt))

        def sem(name):
            return ctx.enter_context(nc.semaphore(name))

        bank_a = ctx.enter_context(nc.psum_tensor("bank_a", [P, 2, S], F32))
        bank_b = ctx.enter_context(nc.psum_tensor("bank_b", [P, 2, S], F32))
        bank_s = ctx.enter_context(nc.psum_tensor("bank_s", [P, 2, S], F32))
        bank_t = ctx.enter_context(nc.psum_tensor("bank_t", [P, S], F32))
        bank_o = ctx.enter_context(nc.psum_tensor("bank_o", [P, S], F32))

        ident = sb("ident", [P, P])
        ident_bf = sb("ident_bf", [P, P], BF16)
        mask_bf = sb("mask_bf", [P, P], BF16)
        mask01 = sb("mask01", [P, P])
        ones = sb("ones", [P, P])
        ones_r = sb("ones_r", [P, P], F32R)
        cols = sb("cols", [P, 2])
        vec_a = sb("vec_a", [P, P])
        vec_b = sb("vec_b", [P, P])
        c_act = sb("c_act", [P, KC])
        gq_scaled = sb("gq_scaled", [P, 1])
        bf_col = sb("bf_col", [H, 1])
        mod = sb("mod", [P, 6 * KC])
        a1 = sb("a1", [P, KC])
        a2 = sb("a2", [P, KC])
        x_sum = sb("x_sum", [P, ST])
        x_root = sb("x_root", [P, ST])
        x_inv = sb("x_inv", [P, ST])
        neg_sel = sb("neg_sel", [P, H])
        f_split = sb("f_split", [P, S], F32R)
        wf_raw = sb("wf_raw", [P, KC, H])
        wf = sb("wf", [P, KC, 2 * H], F32R)
        neg_max = sb("neg_max", [P, 8])
        row_sum = sb("row_sum", [P, 8])
        row_inv = sb("row_inv", [P, 8])
        vg_stats = sb("vg_stats", [P, 2, ST, 6])
        vg_mv = sb("vg_mv", [P, 2, ST, 2])
        vg_root = sb("vg_root", [P, 2, ST])
        vg_inv = sb("vg_inv", [P, 2, ST])
        raw = sb("raw", [P, RAW, 4, PAIR])
        w_hi = sb("w_hi", [P, SPLIT, 2, PAIR], F32R)
        w_lo = sb("w_lo", [P, SPLIT, 2, PAIR], F32R)
        h_hi = sb("h_hi", [P, KC, S], F32R)
        early = ExitStack()
        xhat = sb("xhat", [P, KC, S], F32, early)
        early.close()
        h_lo = sb("h_lo", [P, KC, S], F32R)
        early = ExitStack()
        mod_tile = sb("mod_tile", [P, MRING, 2, GC], F32, early)
        mod_acc = sb("mod_acc", [P, GRPS * 2, GC], F32, early)
        early.close()
        mix_hi = sb("mix_hi", [P, KC, S], F32R)
        mix_lo = sb("mix_lo", [P, KC, S], F32R)
        tmp = sb("tmp", [P, 2, S])
        part = sb("part", [P, 2, S])
        early = ExitStack()
        x_nat = sb("x_nat", [P, ST, D], F32, early)
        early.close()
        early = ExitStack()
        q_t = sb("q_t", [P, 2, S], F32, early)
        k_t = sb("k_t", [P, 2, S], F32, early)
        v_n = sb("v_n", [P, 2, ST, P], F32, early)
        vg_n = sb("vg_n", [P, 2, ST, P], F32, early)
        inner = ExitStack()
        sq_parts = sb("sq_parts", [P, 2, 2, S], F32R, inner)
        inner.close()
        prob = sb("prob", [P, ST, S], F32, early)
        prob_t = sb("prob_t", [P, ST, S], F32, early)
        early.close()
        x1 = sb("x1", [P, KC, S])
        early = ExitStack()
        rows_a = sb("rows_a", [P, P], F32, early)
        rows_b = sb("rows_b", [P, P], F32, early)
        early.close()
        early = ExitStack()
        ws_nat = sb("ws_nat", [P, 2, P], F32, early)
        ws_t = sb("ws_t", [P, 2, P], F32, early)
        bs_all = sb("bs_all", [P, 2, P], F32, early)
        sel_cur = sb("sel_cur", [P, 2, P], F32R, early)
        early.close()
        x_stage = sb("x_stage", [P, ST, PAIR])
        ada_tile = sb("ada_tile", [P, ARING, AB])
        ada_acc = sb("ada_acc", [P, AB])
        inv, sq_acc = part[:, 0, :], part[:, 1, :]
        f_x, f_y = tmp[0:H, 0, :], tmp[0:H, 1, :]
        f_cum, f_ones = part[0:H, 0, :], part[0:H, 1, :]

        consts_made = sem("consts_made")
        ones_rounded = sem("ones_rounded")
        rows_in = sem("rows_in")
        small_in = sem("small_in")
        rows_turned = sem("rows_turned")
        vecs_ready = sem("vecs_ready")
        c_ready = sem("c_ready")
        gq_ready = sem("gq_ready")
        x_in = [sem(f"x_in{i}") for i in range(ST)]
        x_squared = sem("x_squared")
        x_rooted = sem("x_rooted")
        x_inverted = sem("x_inverted")
        x_normed = sem("x_normed")
        x_turned = sem("x_turned")
        xhat_ready = sem("xhat_ready")
        mod_in = [sem(f"mod_in{i}") for i in range(MRING)]
        mod_step = sem("mod_step")
        mod_sums = sem("mod_sums")
        mod_added = sem("mod_added")
        a1_ready = sem("a1_ready")
        h_full = sem("h_full")
        h_hi_ready = sem("h_hi_ready")
        h_ready = sem("h_ready")
        wf_rounded = sem("wf_rounded")
        wf_ready = sem("wf_ready")
        f_sums = sem("f_sums")
        f_biased = sem("f_biased")
        f_act = sem("f_act")
        f_log = sem("f_log")
        f_summed = sem("f_summed")
        f_hi_ready = sem("f_hi_ready")
        f_ready = sem("f_ready")
        f_cleared = sem("f_cleared")
        raw_in = [sem(f"raw_in{i}") for i in range(RAW)]
        w_rounded = sem("w_rounded")
        w_split = sem("w_split")
        slot_used = sem("slot_used")
        ws_in = sem("ws_in")
        bs_in = sem("bs_in")
        ws_turned = sem("ws_turned")
        ws_ready = sem("ws_ready")
        sel_ready = sem("sel_ready")
        squares = sem("squares")
        squares_hi = sem("squares_hi")
        squares_split = sem("squares_split")
        norm_sums = sem("norm_sums")
        norm_root = sem("norm_root")
        norm_inv = sem("norm_inv")
        qk_ready = sem("qk_ready")
        scores = sem("scores")
        maxima = sem("maxima")
        exps = sem("exps")
        sums_inv = sem("sums_inv")
        probs = sem("probs")
        probs_turned = sem("probs_turned")
        probs_t = sem("probs_t")
        v_part = sem("v_part")
        v_turned = sem("v_turned")
        v_ready = sem("v_ready")
        attn_sums = sem("attn_sums")
        attn_hi = sem("attn_hi")
        attn_ready = sem("attn_ready")
        vg_part = sem("vg_part")
        vg_turned = sem("vg_turned")
        vg_stat = sem("vg_stat")
        vg_agg = sem("vg_agg")
        vg_rooted = sem("vg_rooted")
        vg_inverted = sem("vg_inverted")
        vg_ready = sem("vg_ready")
        z_sums = sem("z_sums")
        z_ready = sem("z_ready")
        gate_ready = sem("gate_ready")
        gated = sem("gated")
        sgu_hi = sem("sgu_hi")
        sgu_ready = sem("sgu_ready")
        ada_in = [sem(f"ada_in{i}") for i in range(ARING)]
        ada_step = sem("ada_step")
        ada_sums = sem("ada_sums")
        ada_added = sem("ada_added")
        stage_in = sem("stage_in")
        stage_turned = sem("stage_turned")
        x1_old = sem("x1_old")
        x1_ready = [sem(f"x1_ready{q}") for q in range(2)]
        x1_square = sem("x1_square")
        sq_added = sem("sq_added")
        sq_sums = sem("sq_sums")
        sq_root = sem("sq_root")
        sq_cleared = sem("sq_cleared")
        inv_ready = sem("inv_ready")
        a2_ready = sem("a2_ready")
        h2_scaled = sem("h2_scaled")
        h2_hi = sem("h2_hi")
        h2_ready = sem("h2_ready")
        relu_ready = [sem(f"relu_ready{q}") for q in range(2)]
        ff_square = sem("ff_square")
        ff_hi = sem("ff_hi")
        ff_ready = sem("ff_ready")
        ff_added = [sem(f"ff_added{q}") for q in range(2)]
        y_turned = sem("y_turned")
        y_ready = sem("y_ready")
        y_out = sem("y_out")

        w_in_v = w_in[0].rearrange("(k p) n -> p k n", p=P)
        w_out_v = w_out[0].rearrange("(g h c p) n -> p h g c n", g=2, h=HP, p=P)
        w_ff1_v = w_ff1[0].rearrange("(k p) n -> p k n", p=P)
        w_ff2_v = w_ff2[0].rearrange("(c k p) n -> p c k n", c=FC, p=P)
        ada_v = w_ada[0].rearrange("(k p) (m n) -> k p m n", p=P, m=6)
        ada_flat = w_ada[0].rearrange("(k p) n -> k p n", p=P)
        x_v = x[0].rearrange("(i p) d -> p i d", p=P)
        out_v = out[0].rearrange("(i p) d -> p i d", p=P)
        b_s_v = b_s[0].rearrange("g t -> (g t)")

        block = ctx.enter_context(nc.Block())

        @block.sync
        def _(sp):
            sp.wait_ge(consts_made, 6)
            sp.dma_start(rows_b[0:KC, :], c.rearrange("a (k p) -> (a k) p", p=P)).then_inc(rows_in, 16)
            sp.dma_start(rows_a[0:6 * KC, :], b_ada.rearrange("a (k p) -> (a k) p", p=P)).then_inc(rows_in, 16)
            sp.dma_start(rows_a[6 * KC:7 * KC, :], g_mix.rearrange("a (k p) -> (a k) p", p=P)).then_inc(rows_in, 16)
            sp.dma_start(rows_a[7 * KC:8 * KC, :], g_ffn.rearrange("a (k p) -> (a k) p", p=P)).then_inc(rows_in, 16)
            sp.dma_start(rows_b[KC:KC + G, :], g_sgu[0]).then_inc(rows_in, 16)
            sp.dma_start(rows_b[KC + G:KC + G + 1, :], g_q).then_inc(rows_in, 16)
            sp.dma_start(rows_b[KC + G + 1:KC + G + 2, :], g_k).then_inc(rows_in, 16)
            sp.dma_start(bf_col[:, :], b_f.rearrange("a h -> h a")).then_inc(small_in, 16)
            sp.dma_start(wf_raw[:, :, :], w_in_v[:, :, COL_F:COL_F + H]).then_inc(small_in, 16)
            for i in range(ST):
                sp.dma_start(x_nat[:, i, :], x_v[:, i, :]).then_inc(x_in[i], 16)

            def mod_load(g, k):
                sp.dma_start(mod_tile[:, k % MRING, :, :],
                             ada_v[k, :, 0:2, bass.ds(g * GC, GC)]).then_inc(mod_in[k % MRING], 16)

            for k in range(MRING):
                mod_load(0, k)
            for k in range(MRING, KC):
                sp.wait_ge(mod_step, 2 * (k - MRING + 1))
                mod_load(0, k)
            with sp.Fori(1, GRPS) as g:
                for k in range(KC):
                    sp.wait_ge(mod_step, g * (2 * KC) + 2 * (k - MRING + 1))
                    mod_load(g, k)
            def chunk_load(pair, n, src):
                sp.wait_ge(w_split, pair * SLOTS + 2 * n + 2)
                sp.dma_start(raw[:, n, :, :], src).then_inc(raw_in[n], 32)

            with sp.Fori(0, HP) as hp:
                for j in range(STEP_SLOTS):
                    if j % 2 == 0:
                        col = (0, COL_K, COL_V, COL_VG, COL_U)[j // SLOTS]
                        n = (j % SLOTS) // 2
                        chunk_load(hp * STEP_PAIRS + j // SLOTS, n,
                                   w_in_v[:, 4 * n:4 * n + 4, bass.ds(hp * PAIR + col, PAIR)])
                    if j == 1:
                        sp.wait_ge(ws_turned, START + hp)
                        sp.dma_start(ws_nat[:, :, :], w_s[0].rearrange("g t s -> t g s")[:, bass.ds(hp * 2, 2), :]).then_inc(ws_in, 16)
                    if j == 4:
                        sp.wait_ge(z_ready, START + hp * 2)
                        sp.dma_start(bs_all[:, :, :].rearrange("p g t -> p (g t)"),
                                     b_s_v[bass.ds(hp * PAIR, PAIR)].partition_broadcast(P)).then_inc(bs_in, 16)
            with sp.Fori(0, BODIES) as b:
                for q in range(2):
                    for n in range(4):
                        sp.wait_ge(w_split, (b * 2 + (OUT_PAIR + q)) * SLOTS + 2 * n + 2)
                        for g in range(2):
                            sp.dma_start(raw[:, n, 2 * g:2 * g + 2, :],
                                         w_out_v[:, n, g, :, bass.ds(b * (2 * PAIR) + q * PAIR, PAIR)]).then_inc(raw_in[n], 16)
                        if n == 2:
                            sp.wait_ge(stage_turned, START + b * 4 + 2 * q)
                            sp.wait_ge(scores, START + 8 * HP)
                            sp.wait_ge(z_ready, START + 2 * HP)
                            sp.dma_start(x_stage[:, :, :],
                                         x_v[:, :, bass.ds(b * (2 * PAIR) + q * PAIR, PAIR)]).then_inc(stage_in, 16)

            def ff1_loads(ch, b):
                for q in range(2):
                    for n in range(4):
                        chunk_load(ch * (2 * NPAIR) + (b * 2 + (FF_PAIR + q)), n,
                                   w_ff1_v[:, 4 * n:4 * n + 4, bass.ds(ch * D + (b * (2 * PAIR) + q * PAIR), PAIR)])

            def ff2_loads(ch, b):
                for q in range(2):
                    for n in range(4):
                        chunk_load(ch * (2 * NPAIR) + (b * 2 + (FF_PAIR + NPAIR + q)), n,
                                   w_ff2_v[:, ch, 4 * n:4 * n + 4, bass.ds(b * (2 * PAIR) + q * PAIR, PAIR)])

            with sp.Fori(0, FC) as ch:
                with sp.Fori(0, BODIES) as b:
                    ff1_loads(ch, b)
                with sp.Fori(0, BODIES) as b:
                    ff2_loads(ch, b)
            sp.wait_ge(y_out, START + 16 * NPAIR)

        def h_low(engine, g, t):
            n = bass.ds(g * GRP + t, 1)
            engine.wait_ge(h_full, g * GRP + (t + 1))
            engine.tensor_tensor(h_lo[:, n, :], xhat[:, n, :], h_hi[:, n, :].bitcast(F32), ALU.subtract).then_inc(h_ready, 1)

        @block.gpsimd
        def _(pool):
            for started in (ada_sums, ada_added, ws_turned, z_ready, gate_ready, vg_part, scores, sgu_ready, attn_ready,
                            gated, probs_turned, x1_old, sq_added, x1_square, stage_turned, ff_ready, y_ready, y_turned,
                            y_out, *x1_ready, *relu_ready, *ff_added):
                pool.sem_inc(started, START)
            pool.sem_inc(ada_step, ARING)
            pool.memset(ones[:, :], 1.0).then_inc(consts_made, 1)
            pool.memset(cols[:, 0:1], EPS).then_inc(consts_made, 1)
            pool.memset(cols[:, 1:2], 1.0).then_inc(consts_made, 1)
            pool.memset(mask_bf[:, :], 0.0).then_inc(consts_made, 1)
            pool.memset(neg_sel[:, :], 0.0).then_inc(consts_made, 1)
            pool.memset(rows_b[:, :], 0.0).then_inc(consts_made, 1)
            pool.wait_ge(consts_made, 6)
            pool.affine_select(out=ident[:, :], in_=ones[:, :], compare_op=ALU.is_equal, fill=0.0, base=0,
                               pattern=[[-1, P]], channel_multiplier=1).then_inc(consts_made, 1)
            pool.affine_select(out=mask01[:, :], in_=ones[:, :], compare_op=ALU.is_ge, fill=0.0, base=0,
                               pattern=[[1, P]], channel_multiplier=-1).then_inc(consts_made, 1)
            pool.affine_select(out=mask_bf[:, :], in_=mask_bf[:, :], compare_op=ALU.is_ge, fill=NEG, base=0,
                               pattern=[[-1, P]], channel_multiplier=1).then_inc(consts_made, 1)
            pool.wait_ge(consts_made, 9)
            pool.tensor_copy(ident_bf[:, :], ident[:, :]).then_inc(consts_made, 1)
            for at in (0, 32):
                pool.affine_select(out=neg_sel[:, :], in_=neg_sel[:, :], compare_op=ALU.not_equal, fill=-1.0,
                                   base=-at, pattern=[[-1, H]], channel_multiplier=1).then_inc(consts_made, 1)
                pool.wait_ge(consts_made, 11 + (at > 0))
            with pool.Fori(0, GRPS - 1) as g:
                for t in range(GRP):
                    h_low(pool, g, t)


        @block.scalar
        def _(act):
            def round_slot(pair0, j):
                n = (j % SLOTS) // 2
                act.wait_ge(raw_in[n], pair0 * 32 + 32 * (j // SLOTS + 1))
                act.wait_ge(slot_used, pair0 * SLOTS + (j + 1))
                act.activation(w_hi[:, j % SPLIT, :, :], raw[:, n, 2 * (j % 2):2 * (j % 2) + 2, :],
                               ACT.Copy).then_inc(w_rounded, 1)

            act.wait_ge(consts_made, CONSTS)
            act.wait_ge(vecs_ready, 2)
            act.activation(c_act[:, :], vec_b[:, 0:KC], ACT.Silu).then_inc(c_ready, 1)
            act.wait_ge(small_in, 32)
            act.activation(wf[:, :, 0:H], wf_raw[:, :, :], ACT.Copy).then_inc(wf_rounded, 1)
            for i in range(ST):
                act.wait_ge(x_in[i], 16)
                act.activation(xhat[:, 4 * i:4 * i + 4, :], x_nat[:, i, :].rearrange("p (k n) -> p k n", k=4),
                               ACT.Square, accum_out=x_sum[:, i:i + 1]).then_inc(x_squared, 1)
            act.wait_ge(x_squared, ST)
            act.activation(x_root[:, :], x_sum[:, :], ACT.Sqrt, bias=cols[:, 0:1], scale=1.0 / D).then_inc(x_rooted, 1)
            act.wait_ge(x_inverted, 1)
            for i in range(ST):
                act.activation(x_nat[:, i, :], x_nat[:, i, :], ACT.Copy, scale=x_inv[:, i:i + 1]).then_inc(x_normed, 1)
            with act.Fori(0, KC // 2) as t:
                for a in range(2):
                    act.wait_ge(consts_made, CONSTS)
                    act.wait_ge(x_turned, t * 2 + (a + 1))
                    act.activation(xhat[:, bass.ds(t * 2 + a, 1), :], bank_s[:, a:a + 1, :], ACT.Copy).then_inc(xhat_ready, 1)

            def h_high(g, full):
                act.wait_ge(a1_ready, g + 1)
                act.wait_ge(consts_made, CONSTS)
                for t in range(GRP):
                    if full and t >= 1:
                        act.wait_ge(h_hi_ready, g * GRP + t)
                    act.wait_ge(consts_made, CONSTS)
                    n = bass.ds(g * GRP + t, 1)
                    act.activation(h_hi[:, n, :], xhat[:, n, :], ACT.Identity, scale=a1[:, n], bias=mod[:, n]).then_inc(h_hi_ready, 1)
                    if full and t >= 1:
                        n = bass.ds(g * GRP + (t - 1), 1)
                        act.activation(xhat[:, n, :], xhat[:, n, :], ACT.Identity, scale=a1[:, n], bias=mod[:, n]).then_inc(h_full, 1)

            with act.Fori(0, GRPS - 1) as g:
                h_high(g, True)
            h_high(GRPS - 1, False)
            for j in range(LEAD):
                round_slot(0, j)
            act.wait_ge(f_biased, 1)
            act.activation(f_y, f_x, ACT.Abs).then_inc(f_act, 1)
            act.wait_ge(f_act, 1)
            act.activation(f_y, f_y, ACT.Exp, scale=-1.0).then_inc(f_act, 1)
            act.wait_ge(f_act, 2)
            act.activation(f_y, f_y, ACT.Ln, bias=cols[0:H, 1:2]).then_inc(f_act, 1)

            def squares_of(hp, e0, bank):
                for a in range(2):
                    act.activation(tmp[:, a, :], bank[:, a, :], ACT.Square).then_inc(squares, 1)
                act.wait_ge(probs_turned, START + hp * 8)
                for a in range(2):
                    act.wait_ge(squares, hp * 4 + (e0 + a + 1))
                    act.activation(sq_parts[:, 0, a, :], tmp[:, a, :], ACT.Copy).then_inc(squares_hi, 1)

            def roots_of(hp, e0):
                for e in (e0, e0 + 1):
                    act.wait_ge(norm_sums, hp * 4 + (e + 1))
                    src = (bank_s[:, 0, :], bank_s[:, 1, :], bank_t[:, :], bank_o[:, :])[e]
                    act.activation(tmp[:, e % 2, :], src, ACT.Sqrt, bias=cols[:, 0:1], scale=1.0 / DH).then_inc(norm_root, 1)

            def ada_loads(block, j, steps):
                for at, slot in enumerate(steps):
                    if (steps[at - ARING] + 1 if at >= ARING else 0) != j:
                        continue
                    blk, k = at // KC, at % KC
                    act.wait_ge(ada_step, (block + blk) * KC + (k + 1))
                    act.dma_start(ada_tile[:, k % ARING, :],
                                  ada_flat[k, :, bass.ds(block * AB + (GATE1 * P + blk * AB), AB)]
                                  ).then_inc(ada_in[k % ARING], 16)

            def exp_of(hp, t):
                n = P * (t % ST + 1)
                act.wait_ge(maxima, hp * 8 + (t + 1))
                act.wait_ge(probs_turned, START + hp * 8 + max(t - ST + 1, 0))
                act.activation(prob[:, t % ST, 0:n], bank_s[:, t % 2, 0:n], ACT.Exp, bias=neg_max[:, t:t + 1],
                               accum_out=row_sum[:, t:t + 1]).then_inc(exps, 1)

            def copy_prob_t(hp, t):
                i = t % ST
                act.wait_ge(probs_turned, START + hp * 8 + (t + 1))
                if t >= ST:
                    act.wait_ge(attn_sums, hp * 2 + 1)
                act.activation(prob_t[:, 0:i + 1, P * i:P * (i + 1)],
                               bank_t[:, 0:P * (i + 1)].rearrange("p (j q) -> p j q", q=P), ACT.Copy).then_inc(probs_t, 1)

            def slot_done(pair0, j):
                act.wait_ge(slot_used, pair0 * SLOTS + (j + 1 + SPLIT))

            with act.Fori(0, HP) as hp:
                pair0 = hp * STEP_PAIRS
                for j in range(STEP_SLOTS):
                    round_slot(pair0, j + LEAD)
                    ada_loads(hp * 2, j, ADA_IN)
                    if j == 7:
                        slot_done(pair0, j)
                        act.wait_ge(sgu_ready, START + hp * 2)
                        act.wait_ge(f_ready, 1)
                        squares_of(hp, 0, bank_a)
                    if j == 10:
                        roots_of(hp, 0)
                    if j == 15:
                        slot_done(pair0, j)
                        act.wait_ge(qk_ready, hp * 4 + 2)
                        squares_of(hp, 2, bank_b)
                    if j == 19:
                        roots_of(hp, 2)
                    if j - 4 in SCORE_AT:
                        copy_prob_t(hp, SCORE_AT.index(j - 4))
                    if j - 1 in SCORE_AT:
                        exp_of(hp, SCORE_AT.index(j - 1))
                    if j == 23:
                        slot_done(pair0, j)
                        act.wait_ge(gated, START + hp * 2)
                        act.wait_ge(f_ready, 1)
                        for a in range(2):
                            act.activation(part[:, a, :], bank_a[:, a, :], ACT.Copy).then_inc(v_part, 1)
                    if j in (25, 27):
                        a = (j - 25) // 2
                        act.wait_ge(v_turned, hp * 2 + (a + 1))
                        act.activation(v_n[:, a, :, :], bank_o[:, :].rearrange("p (i d) -> p i d", d=P),
                                       ACT.Copy).then_inc(v_ready, 1)
                    if j in (29, 35):
                        a = (j - 29) // 6
                        act.wait_ge(consts_made, CONSTS)
                        act.wait_ge(attn_sums, hp * 2 + (a + 1))
                        act.activation(mix_hi[:, bass.ds(hp * 4 + a, 1), :].rearrange("p k n -> p (k n)"),
                                       bank_o[:, :], ACT.Copy).then_inc(attn_hi, 1)
                    if j == 31:
                        slot_done(pair0, j)
                        act.wait_ge(v_turned, hp * 2 + 2)
                        for a in range(2):
                            act.activation(part[:, a, :], bank_b[:, a, :], ACT.Gelu_apprx_tanh).then_inc(vg_part, 1)
                    if j in (35, 37):
                        a = (j - 35) // 2
                        act.wait_ge(vg_agg, hp * 2 + (a + 1))
                        act.activation(vg_root[:, a, :], vg_mv[:, a, :, 1], ACT.Sqrt, bias=cols[:, 0:1]).then_inc(vg_rooted, 1)
                    if j == 39:
                        slot_done(pair0, j)
                        for a in range(2):
                            act.activation(tmp[:, a, :], bank_s[:, a, :], ACT.Gelu_apprx_tanh).then_inc(gate_ready, 1)
                        for a in range(2):
                            act.wait_ge(consts_made, CONSTS)
                            act.wait_ge(gated, START + hp * 2 + (a + 1))
                            act.activation(mix_hi[:, bass.ds(hp * 4 + (2 + a), 1), :], tmp[:, a:a + 1, :],
                                           ACT.Copy).then_inc(sgu_hi, 1)

            with act.Fori(0, BODIES) as b:
                pair0 = b * 2 + OUT_PAIR
                for j in range(2 * SLOTS):
                    q = j // SLOTS
                    round_slot(pair0, j + LEAD)
                    ada_loads(b + OUT_BLOCK, j, ADA_BODY)
                    if j % SLOTS == 5:
                        for a in range(2):
                            act.wait_ge(consts_made, CONSTS)
                            act.wait_ge(stage_turned, START + b * 4 + (2 * q + a + 1))
                            act.activation(x1[:, bass.ds(b * 4 + (2 * q + a), 1), :], bank_s[:, a:a + 1, :],
                                           ACT.Copy).then_inc(x1_old, 1)
            act.wait_ge(sq_sums, 1)
            act.activation(inv[:, :], bank_o[:, :], ACT.Sqrt, bias=cols[:, 0:1], scale=1.0 / D).then_inc(sq_root, 1)

            def h2_high(slot):
                for n in (2 * slot, 2 * slot + 1):
                    act.wait_ge(h2_scaled, n + 1)
                    act.activation(h_hi[:, n, :], tmp[:, n % 2, :], ACT.Identity,
                                   bias=mod[:, SHIFT2 + n:SHIFT2 + n + 1]).then_inc(h2_hi, 1)

            h2_high(0)

            def ff1_body(ch, b, ada=False, first=False):
                pair0 = ch * (2 * NPAIR) + (b * 2 + FF_PAIR)
                for j in range(2 * SLOTS):
                    if first and j + 1 < SLOTS:
                        h2_high(j + 1)
                    round_slot(pair0, j + LEAD)
                    if ada:
                        ada_loads(b + FF_BLOCK, j, ADA_FIRST if first else ADA_BODY)
                    if j % SLOTS == 7:
                        q = j // SLOTS
                        bank = (bank_a, bank_b)[q]
                        n0 = ch * KC + (b * 4 + 2 * q)
                        slot_done(pair0, j)
                        act.wait_ge(ff_ready, START + n0)
                        act.wait_ge(h2_ready, KC)
                        act.activation(tmp[:, :, :], bank[:, :, :], ACT.Relu).then_inc(relu_ready[q], 1)
                        for a in range(2):
                            act.wait_ge(consts_made, CONSTS)
                            act.wait_ge(ff_square, n0 + (a + 1))
                            act.activation(mix_hi[:, bass.ds(b * 4 + (2 * q + a), 1), :], tmp[:, a:a + 1, :],
                                           ACT.Copy).then_inc(ff_hi, 1)

            def copy_out(b, n):
                act.wait_ge(y_turned, START + n + 1)
                act.wait_ge(y_out, START + n * 16)
                act.activation(x_stage[:, :, :].rearrange("p i n -> p (i n)"),
                               bank_s[:, :, :].rearrange("p b n -> p (b n)"), ACT.Copy).then_inc(y_ready, 1)
                act.wait_ge(y_ready, START + n + 1)
                act.dma_start(out_v[:, :, bass.ds(n * PAIR, PAIR)], x_stage[:, :, :]).then_inc(y_out, 16)

            def ff2_body(ch, b, last=False, first_out=True, store=False):
                pair0 = ch * (2 * NPAIR) + (b * 2 + (FF_PAIR + NPAIR))
                for j in range(2 * SLOTS):
                    if not (last and j + LEAD >= 2 * SLOTS):
                        round_slot(pair0, j + LEAD)
                    if store and j == 3 and not first_out:
                        copy_out(b, b * 2 - 1)
                    if store and j == 11:
                        copy_out(b, b * 2)

            ff1_body(0, 0, ada=True, first=True)
            with act.Fori(1, BODIES) as b:
                ff1_body(0, b, ada=True)
            with act.Fori(0, FC - 1) as ch:
                with act.Fori(0, BODIES) as b:
                    ff2_body(ch, b)
                with act.Fori(0, BODIES) as b:
                    ff1_body(ch + 1, b)
            ff2_body(FC - 1, 0, store=True)
            with act.Fori(1, BODIES - 1) as b:
                ff2_body(FC - 1, b, first_out=False, store=True)
            ff2_body(FC - 1, BODIES - 1, last=True, first_out=False, store=True)
            copy_out(BODIES, NPAIR - 1)

        @block.vector
        def _(dve):
            def split_slot(pair0, j):
                n = (j % SLOTS) // 2
                dve.wait_ge(w_rounded, pair0 * SLOTS + (j + 1))
                dve.tensor_tensor(w_lo[:, j % SPLIT, :, :], raw[:, n, 2 * (j % 2):2 * (j % 2) + 2, :],
                                  w_hi[:, j % SPLIT, :, :].bitcast(F32), ALU.subtract).then_inc(w_split, 1)

            dve.memset(f_split[:, :].bitcast(F32), 0.0).then_inc(w_split, 2 * RAW)
            dve.memset(f_ones, 1.0).then_inc(f_cleared, 1)
            dve.wait_ge(consts_made, CONSTS)
            dve.tensor_copy(ones_r[:, :], ones[:, :]).then_inc(ones_rounded, 1)
            dve.wait_ge(rows_turned, 1)
            dve.tensor_copy(vec_b[:, :], bank_o[:, P:2 * P]).then_inc(vecs_ready, 1)
            dve.tensor_copy(vec_a[:, :], bank_o[:, 0:P]).then_inc(vecs_ready, 1)
            dve.wait_ge(vecs_ready, 2)
            dve.tensor_scalar(gq_scaled[:, :], vec_b[:, KC + G:KC + G + 1], float(DH) ** -0.5, None,
                              ALU.mult).then_inc(gq_ready, 1)
            dve.wait_ge(x_rooted, 1)
            dve.reciprocal(x_inv[:, :], x_root[:, :]).then_inc(x_inverted, 1)
            dve.wait_ge(c_ready, 1)

            dve.wait_ge(wf_rounded, 1)
            dve.tensor_tensor(wf[:, :, H:2 * H], wf_raw[:, :, :], wf[:, :, 0:H].bitcast(F32), ALU.subtract).then_inc(wf_ready, 1)

            def mod_group_step(g, k):
                dve.wait_ge(mod_in[k % MRING], g * (16 * KC // MRING) + 16 * (k // MRING + 1))
                for m in range(2):
                    acc = mod_acc[:, bass.ds(g * 2 + m, 1), :]
                    tile = mod_tile[:, k % MRING, m:m + 1, :]
                    if k == 0:
                        dve.tensor_scalar(acc, tile, c_act[:, k:k + 1], None, ALU.mult).then_inc(mod_step, 1)
                    else:
                        dve.wait_ge(mod_step, g * (2 * KC) + (2 * k + m - 1))
                        dve.scalar_tensor_tensor(out=acc, in0=tile, scalar=c_act[:, k:k + 1],
                                                 in1=acc, op0=ALU.mult, op1=ALU.add).then_inc(mod_step, 1)

            def mod_group_add(g):
                dve.wait_ge(mod_sums, g + 1)
                for m in range(2):
                    at = bass.ds(g * GRP + m * KC, GRP)
                    dve.tensor_tensor(mod[:, at], bank_t[:, m * GRP:(m + 1) * GRP], vec_a[:, at],
                                      ALU.add).then_inc(mod_added, 1)
                dve.wait_ge(mod_added, g * 2 + 2)
                dve.scalar_tensor_tensor(out=a1[:, bass.ds(g * GRP, GRP)], in0=mod[:, bass.ds(g * GRP + SCALE1, GRP)],
                                         scalar=1.0, in1=vec_a[:, bass.ds(g * GRP + 6 * KC, GRP)],
                                         op0=ALU.add, op1=ALU.mult).then_inc(a1_ready, 1)

            def h_of(g, t):
                n = bass.ds(g * GRP + t, 1)
                dve.wait_ge(h_hi_ready, g * GRP + (t + 1))
                dve.wait_ge(h_full, g * GRP + t)
                dve.tensor_scalar(xhat[:, n, :], xhat[:, n, :], a1[:, n], mod[:, n], ALU.mult, ALU.add).then_inc(h_full, 1)

            for k in range(KC):
                mod_group_step(0, k)
            with dve.Fori(1, GRPS) as g:
                for k in range(KC):
                    mod_group_step(g, k)
                    if k == 3:
                        mod_group_add(g - 1)
                    if k == 10:
                        h_of(g - 1, GRP - 1)
            mod_group_add(GRPS - 1)
            dve.wait_ge(h_ready, (GRPS - 1) * GRP)
            for t in range(GRP):
                h_of(GRPS - 1, t)
                h_low(dve, GRPS - 1, t)
            for j in range(LEAD):
                split_slot(0, j)
            dve.wait_ge(f_sums, GRPS)
            dve.tensor_scalar(f_x, bank_s[0:H, 0, :], bf_col[:, 0:1], None, ALU.add).then_inc(f_biased, 1)
            dve.wait_ge(f_act, 3)
            dve.scalar_tensor_tensor(out=f_x, in0=f_x, scalar=0.0, in1=f_y, op0=ALU.min, op1=ALU.subtract).then_inc(f_log, 1)
            dve.wait_ge(f_log, 1)
            dve.tensor_tensor_scan(f_cum, f_ones, f_x, 0.0, ALU.mult, ALU.add).then_inc(f_summed, 1)
            dve.wait_ge(f_summed, 1)
            dve.tensor_copy(f_split[0:H, :], f_cum).then_inc(f_hi_ready, 1)
            dve.wait_ge(f_hi_ready, 1)
            dve.tensor_tensor(f_split[32:32 + H, :], f_cum, f_split[0:H, :].bitcast(F32), ALU.subtract).then_inc(f_ready, 1)

            def norm_of(hp, e, bank):
                a = e % 2
                dve.wait_ge(norm_root, hp * 4 + (e + 1))
                dve.reciprocal(tmp[:, a, :], tmp[:, a, :]).then_inc(norm_inv, 1)
                dve.wait_ge(norm_inv, hp * 4 + (e + 1))
                dst, g = ((q_t, gq_scaled[:, 0:1]), (k_t, vec_b[:, KC + G + 1:KC + G + 2]))[e // 2]
                dve.scalar_tensor_tensor(out=dst[:, a, :], in0=bank[:, a, :], scalar=g, in1=tmp[:, a, :],
                                         op0=ALU.mult, op1=ALU.mult).then_inc(qk_ready, 1)

            def ada_steps(block, j, steps):
                for at, slot in enumerate(steps):
                    if slot != j:
                        continue
                    blk, k = at // KC, at % KC
                    dve.wait_ge(ada_in[k % ARING], block * (16 * KC // ARING) + (blk * (16 * KC // ARING) + 16 * (k // ARING + 1)))
                    if k == 0:
                        dve.wait_ge(ada_sums, START + block + blk)
                        dve.tensor_scalar(ada_acc[:, :], ada_tile[:, k % ARING, :], c_act[:, k:k + 1], None,
                                          ALU.mult).then_inc(ada_step, 1)
                    else:
                        dve.wait_ge(ada_step, ARING + block * KC + (blk * KC + k))
                        dve.scalar_tensor_tensor(out=ada_acc[:, :], in0=ada_tile[:, k % ARING, :], scalar=c_act[:, k:k + 1],
                                                 in1=ada_acc[:, :], op0=ALU.mult, op1=ALU.add).then_inc(ada_step, 1)

            def ada_add(block, src):
                dve.wait_ge(ada_sums, START + block + 1)
                at = bass.ds(block * ABT + GATE1, ABT)
                dve.tensor_tensor(mod[:, at], src[:, 0:ABT], vec_a[:, at], ALU.add).then_inc(ada_added, 1)

            def max_of(hp, t):
                dve.wait_ge(scores, START + hp * 8 + (t + 1))
                dve.reduce_max(neg_max[:, t:t + 1], bank_s[:, t % 2, 0:P * (t % ST + 1)], AX_X,
                               negate=True).then_inc(maxima, 1)

            def scale_of(hp, t):
                n = P * (t % ST + 1)
                dve.wait_ge(exps, hp * 8 + (t + 1))
                dve.reciprocal(row_inv[:, t:t + 1], row_sum[:, t:t + 1]).then_inc(sums_inv, 1)
                dve.wait_ge(sums_inv, hp * 8 + (t + 1))
                dve.tensor_scalar(prob[:, t % ST, 0:n], prob[:, t % ST, 0:n], row_inv[:, t:t + 1], None,
                                  ALU.mult).then_inc(probs, 1)

            def vg_norm_stats(hp, a):
                src = (bank_t, bank_o)[a]
                dve.wait_ge(vg_turned, hp * 2 + (a + 1))
                for i in range(ST):
                    dve.bn_stats(vg_stats[:, a, i, :], src[:, P * i:P * (i + 1)]).then_inc(vg_stat, 1)
                dve.wait_ge(consts_made, CONSTS)
                dve.wait_ge(vg_stat, hp * (2 * ST) + ST * (a + 1))
                for i in range(ST):
                    ins = dve.bn_aggr(vg_mv[:, a, i, :], vg_stats[:, a, i, :])
                ins.then_inc(vg_agg, 1)

            def vg_norm(hp, a):
                src = (bank_t, bank_o)[a]
                dve.wait_ge(vg_rooted, hp * 2 + (a + 1))
                dve.reciprocal(vg_inv[:, a, :], vg_root[:, a, :]).then_inc(vg_inverted, 1)
                dve.wait_ge(vg_inverted, hp * 2 + (a + 1))
                for i in range(ST):
                    ins = dve.tensor_scalar(vg_n[:, a, i, :], src[:, P * i:P * (i + 1)], vg_mv[:, a, i, 0:1],
                                            vg_inv[:, a, i:i + 1], ALU.subtract, ALU.mult)
                ins.then_inc(vg_ready, 1)

            with dve.Fori(0, HP) as hp:
                pair0 = hp * STEP_PAIRS
                for j in range(STEP_SLOTS):
                    split_slot(pair0, j + LEAD)
                    ada_steps(hp * 2, j, ADA_IN)
                    if j == 0:
                        dve.wait_ge(consts_made, CONSTS)
                        dve.wait_ge(scores, START + hp * 8)
                        dve.tensor_copy(sel_cur[:, :, :], neg_sel[:, bass.ds(hp * 2, 2)].unsqueeze(2).to_broadcast([P, 2, P])
                                        ).then_inc(sel_ready, 1)
                    if j == 4:
                        dve.wait_ge(ws_turned, START + hp + 1)
                        for a in range(2):
                            dve.tensor_tensor(ws_t[:, a, :], bank_t[:, P * a:P * (a + 1)], mask01[:, :], ALU.mult).then_inc(ws_ready, 1)
                    if j in (8, 16):
                        for a in range(2):
                            dve.wait_ge(squares_hi, hp * 4 + (j // SLOTS * 2 + a - 1))
                            dve.tensor_tensor(sq_parts[:, 1, a, :], tmp[:, a, :], sq_parts[:, 0, a, :].bitcast(F32),
                                              ALU.subtract).then_inc(squares_split, 1)
                    if j in (10, 12):
                        norm_of(hp, (j - 10) // 2, bank_a)
                    if j in (19, 21):
                        norm_of(hp, 2 + (j - 19) // 2, bank_b)
                    if j == 21:
                        ada_add(hp * 2, bank_t)
                    if j - 1 in SCORE_AT:
                        max_of(hp, SCORE_AT.index(j - 1))
                    if j - 2 in SCORE_AT:
                        scale_of(hp, SCORE_AT.index(j - 2))
                    if j in (29, 35):
                        a = (j - 29) // 6
                        dve.wait_ge(attn_hi, hp * 2 + (a + 1))
                        m = bass.ds(hp * 4 + a, 1)
                        dve.tensor_tensor(mix_lo[:, m, :].rearrange("p k n -> p (k n)"), bank_o[:, :],
                                          mix_hi[:, m, :].rearrange("p k n -> p (k n)").bitcast(F32),
                                          ALU.subtract).then_inc(attn_ready, 1)
                    if j in (35, 37):
                        vg_norm_stats(hp, (j - 35) // 2)
                    if j in (36, 38):
                        vg_norm(hp, (j - 36) // 2)
                    if j == 39:
                        ada_add(hp * 2 + 1, bank_a[:, 0, :])
                        dve.wait_ge(bs_in, hp * 16 + 16)
                        for a in range(2):
                            dve.wait_ge(z_sums, hp * 2 + (a + 1))
                            dve.scalar_tensor_tensor(out=part[:, a, :].rearrange("p (i t) -> p i t", t=P),
                                                     in0=(bank_t, bank_o)[a][:, :].rearrange("p (i t) -> p i t", t=P),
                                                     scalar=vec_b[:, bass.ds(hp * 2 + (KC + a), 1)],
                                                     in1=bs_all[:, a:a + 1, :].to_broadcast([P, ST, P]),
                                                     op0=ALU.mult, op1=ALU.add).then_inc(z_ready, 1)
                    if j == 39:
                        dve.wait_ge(z_ready, START + hp * 2 + 2)
                        for a in range(2):
                            dve.wait_ge(gate_ready, START + hp * 2 + (a + 1))
                            dve.tensor_tensor(tmp[:, a, :], tmp[:, a, :], part[:, a, :], ALU.mult).then_inc(gated, 1)
                        for a in range(2):
                            m = bass.ds(hp * 4 + (2 + a), 1)
                            dve.wait_ge(sgu_hi, hp * 2 + (a + 1))
                            dve.tensor_tensor(mix_lo[:, m, :], tmp[:, a:a + 1, :], mix_hi[:, m, :].bitcast(F32),
                                              ALU.subtract).then_inc(sgu_ready, 1)

            dve.wait_ge(gated, START + 2 * HP)
            dve.memset(sq_acc[:, :], 0.0).then_inc(sq_cleared, 1)
            dve.wait_ge(sgu_ready, START + 2 * HP)
            dve.memset(tmp[:, :, :], 0.0).then_inc(sq_cleared, 1)
            dve.wait_ge(sq_cleared, 2)
            with dve.Fori(0, BODIES) as b:
                pair0 = b * 2 + OUT_PAIR
                for j in range(2 * SLOTS):
                    split_slot(pair0, j + LEAD)
                    ada_steps(b + OUT_BLOCK, j, ADA_BODY)
                    if j % SLOTS == 5:
                        for a in range(2):
                            n0 = b * 4 + (2 * (j // SLOTS) + a)
                            dve.wait_ge(x1_square, START + b * 4 + 2 * (j // SLOTS))
                            dve.wait_ge(sq_added, START + n0)
                            dve.tensor_tensor(sq_acc[:, :], sq_acc[:, :], tmp[:, a, :], ALU.add).then_inc(sq_added, 1)
                    if j % SLOTS == 7:
                        q = j // SLOTS
                        bank = (bank_a, bank_b)[q]
                        dve.wait_ge(slot_used, pair0 * SLOTS + (j + 1 + SPLIT))
                        dve.wait_ge(ada_added, START + OUT_BLOCK)
                        for a in range(2):
                            n0 = b * 4 + (2 * q + a)
                            n = bass.ds(n0, 1)
                            dve.wait_ge(x1_old, START + (n0 + 1))
                            dve.scalar_tensor_tensor(out=x1[:, n, :], in0=bank[:, a:a + 1, :],
                                                     scalar=mod[:, bass.ds(b * 4 + (GATE1 + 2 * q + a), 1)],
                                                     in1=x1[:, n, :], op0=ALU.mult, op1=ALU.add).then_inc(x1_ready[q], 1)
                            dve.wait_ge(x1_ready[q], START + b * 2 + (a + 1))
                            dve.wait_ge(sq_added, START + (n0 + 1))
                            dve.tensor_tensor(tmp[:, a:a + 1, :], x1[:, n, :], x1[:, n, :], ALU.mult).then_inc(x1_square, 1)
                    if j == 15:
                        ada_add(b + OUT_BLOCK, bank_t)
            dve.wait_ge(ada_added, START + FF_BLOCK)
            dve.scalar_tensor_tensor(out=a2[:, :], in0=mod[:, SCALE2:SCALE2 + KC], scalar=1.0,
                                     in1=vec_a[:, 7 * KC:8 * KC], op0=ALU.add, op1=ALU.mult).then_inc(a2_ready, 1)
            dve.wait_ge(sq_root, 1)
            dve.reciprocal(inv[:, :], inv[:, :]).then_inc(inv_ready, 1)
            dve.wait_ge(inv_ready, 1)
            dve.wait_ge(a2_ready, 1)

            def h2_low(slot):
                for n in (2 * slot, 2 * slot + 1):
                    if n >= 2:
                        dve.wait_ge(h2_ready, n - 1)
                    dve.scalar_tensor_tensor(out=tmp[:, n % 2, :], in0=x1[:, n, :], scalar=a2[:, n:n + 1], in1=inv[:, :],
                                             op0=ALU.mult, op1=ALU.mult).then_inc(h2_scaled, 1)
                for n in (2 * slot, 2 * slot + 1):
                    dve.wait_ge(h2_hi, n + 1)
                    dve.scalar_tensor_tensor(out=h_lo[:, n, :], in0=tmp[:, n % 2, :], scalar=mod[:, SHIFT2 + n:SHIFT2 + n + 1],
                                             in1=h_hi[:, n, :].bitcast(F32), op0=ALU.add, op1=ALU.subtract).then_inc(h2_ready, 1)

            h2_low(0)

            def ff1_body(ch, b, ada=False, first=False):
                pair0 = ch * (2 * NPAIR) + (b * 2 + FF_PAIR)
                for j in range(2 * SLOTS):
                    if first and j + 1 < SLOTS:
                        h2_low(j + 1)
                    split_slot(pair0, j + LEAD)
                    if ada:
                        ada_steps(b + FF_BLOCK, j, ADA_FIRST if first else ADA_BODY)
                        if j == 15:
                            ada_add(b + FF_BLOCK, bank_t)
                    if j % SLOTS == 7:
                        q = j // SLOTS
                        n0 = ch * KC + (b * 4 + 2 * q)
                        dve.wait_ge(relu_ready[q], START + ch * BODIES + (b + 1))
                        for a in range(2):
                            dve.tensor_tensor(tmp[:, a, :], tmp[:, a, :], tmp[:, a, :], ALU.mult).then_inc(ff_square, 1)
                        for a in range(2):
                            m = bass.ds(b * 4 + (2 * q + a), 1)
                            dve.wait_ge(ff_hi, n0 + (a + 1))
                            dve.tensor_tensor(mix_lo[:, m, :], tmp[:, a:a + 1, :], mix_hi[:, m, :].bitcast(F32),
                                              ALU.subtract).then_inc(ff_ready, 1)

            def ff2_body(ch, b, last=False, final=False):
                pair0 = ch * (2 * NPAIR) + (b * 2 + (FF_PAIR + NPAIR))
                for j in range(2 * SLOTS):
                    if not (last and j + LEAD >= 2 * SLOTS):
                        split_slot(pair0, j + LEAD)
                    if j % SLOTS == 7:
                        q = j // SLOTS
                        bank = (bank_a, bank_b)[q]
                        dve.wait_ge(slot_used, pair0 * SLOTS + (j + 1 + SPLIT))
                        dve.wait_ge(ada_added, START + FF_BLOCK + BODIES)
                        if final:
                            dve.wait_ge(y_turned, START + b * 2 + q)
                        for a in range(2):
                            n = bass.ds(b * 4 + (2 * q + a), 1)
                            dve.scalar_tensor_tensor(out=part[:, a:a + 1, :] if final else x1[:, n, :],
                                                     in0=bank[:, a:a + 1, :],
                                                     scalar=mod[:, bass.ds(b * 4 + (GATE2 + 2 * q + a), 1)],
                                                     in1=x1[:, n, :], op0=ALU.mult, op1=ALU.add).then_inc(ff_added[q], 1)

            ff1_body(0, 0, ada=True, first=True)
            with dve.Fori(1, BODIES) as b:
                ff1_body(0, b, ada=True)
            with dve.Fori(0, FC - 1) as ch:
                with dve.Fori(0, BODIES) as b:
                    ff2_body(ch, b)
                with dve.Fori(0, BODIES) as b:
                    ff1_body(ch + 1, b)
            with dve.Fori(0, BODIES - 1) as b:
                ff2_body(FC - 1, b, final=True)
            ff2_body(FC - 1, BODIES - 1, last=True, final=True)

        @block.tensor
        def _(pe):
            def product(dst, w_slot, kk, a, act_k, hi, lo, first, last):
                wh = w_hi[:, w_slot, kk, P * a:P * (a + 1)]
                wl = w_lo[:, w_slot, kk, P * a:P * (a + 1)]
                pe.matmul(dst, lhsT=wh, rhs=hi[:, act_k, :], start=first, stop=False)
                pe.matmul(dst, lhsT=wh, rhs=lo[:, act_k, :], start=False, stop=False)
                return pe.matmul(dst, lhsT=wl, rhs=hi[:, act_k, :], start=False, stop=last)

            def slot(pair0, j, bank, hi, lo):
                pe.wait_ge(w_split, pair0 * SLOTS + (j + 1 + 2 * RAW))
                for kk in range(2):
                    k = 2 * (j % SLOTS) + kk
                    for a in range(2):
                        ins = product(bank[:, a, :], j % SPLIT, kk, a, k, hi, lo, k == 0, k == KC - 1)
                ins.then_inc(slot_used, 1)

            pe.wait_ge(consts_made, CONSTS)
            pe.wait_ge(rows_in, 16 * 7)
            pe.transpose(bank_o[:, P:2 * P], rows_b[:, :], ident[:, :]).then_inc(slot_used, SPLIT)
            pe.transpose(bank_o[:, 0:P], rows_a[:, :], ident[:, :]).then_inc(rows_turned, 1)
            pe.wait_ge(x_normed, ST)
            for t in range(KC):
                if t >= 2:
                    pe.wait_ge(xhat_ready, t - 1)
                for i in range(ST):
                    ins = pe.transpose(bank_s[:, t % 2, P * i:P * (i + 1)], x_nat[:, i, P * t:P * (t + 1)], ident[:, :])
                ins.then_inc(x_turned, 1)

            def column_sums(acc, n, dst):
                for t in range(n):
                    ins = pe.matmul(dst[:, t:t + 1], lhsT=acc[:, P * t:P * (t + 1)], rhs=ones[:, 0:1], start=True, stop=True)
                return ins

            def f_logits(g):
                pe.wait_ge(wf_ready, 1)
                pe.wait_ge(xhat_ready, KC)
                for k in range(g * GRP, (g + 1) * GRP):
                    pe.wait_ge(h_ready, k + 1)
                    for w, act_h in ((0, h_hi), (0, h_lo), (H, h_hi)):
                        ins = pe.matmul(bank_s[0:H, 0, :], lhsT=wf[:, k, w:w + H], rhs=act_h[:, k, :],
                                        start=(k == 0 and w == 0 and act_h is h_hi), stop=(k == KC - 1 and w == H))
                ins.then_inc(f_sums, 1)

            for g in range(GRPS):
                if g >= 1:
                    f_logits(g - 1)
                    pe.wait_ge(mod_added, 2 * g)
                for m in range(2):
                    pe.wait_ge(mod_step, (g + 1) * (2 * KC) - 1 + m)
                    ins = column_sums(mod_acc[:, 2 * g + m, :], GRP, bank_t[:, m * GRP:(m + 1) * GRP])
                ins.then_inc(mod_sums, 1)
            f_logits(GRPS - 1)

            def head_slot_tasks(hp, j):
                if j == 3:
                    pe.wait_ge(ws_in, hp * 16 + 16)
                    pe.wait_ge(z_ready, START + hp * 2)
                    for a in range(2):
                        ins = pe.transpose(bank_t[:, P * a:P * (a + 1)], ws_nat[:, a, :], ident[:, :])
                    ins.then_inc(ws_turned, 1)
                if j in (9, 18):
                    for a in range(2):
                        e = 2 * (j // SLOTS - 1) + a
                        pe.wait_ge(squares_split, hp * 4 + (e + 1))
                        if e == 0:
                            pe.wait_ge(ones_rounded, 1)
                            pe.wait_ge(gate_ready, START + hp * 2)
                            pe.wait_ge(f_biased, 1)
                        if e == 2:
                            pe.wait_ge(ws_ready, hp * 2 + 2)
                        if e == 3:
                            pe.wait_ge(z_ready, START + hp * 2)
                        dst = (bank_s[:, 0, :], bank_s[:, 1, :], bank_t[:, :], bank_o[:, :])[e]
                        pe.matmul(dst, lhsT=ones_r[:, :], rhs=sq_parts[:, 0, a, :], start=True, stop=False)
                        pe.matmul(dst, lhsT=ones_r[:, :], rhs=sq_parts[:, 1, a, :], start=False, stop=True).then_inc(norm_sums, 1)
                if j == 20:
                    pe.wait_ge(norm_root, hp * 4 + 3)
                    pe.wait_ge(ada_step, ARING + hp * (2 * KC) + KC)
                    column_sums(ada_acc, ABT, bank_t).then_inc(ada_sums, 1)
                if j in SCORE_AT:
                    t = SCORE_AT.index(j)
                    a, i = t // ST, t % ST
                    n = P * (i + 1)
                    dst = bank_s[:, t % 2, :]
                    pe.wait_ge(qk_ready, hp * 4 + (3 + a))
                    if t < 2:
                        pe.wait_ge(norm_root, hp * 4 + 2)
                    else:
                        pe.wait_ge(exps, hp * 8 + (t - 1))
                    if t == 0:
                        pe.wait_ge(sel_ready, hp + 1)
                        pe.wait_ge(f_ready, 1)
                    pe.matmul(dst[:, 0:n], lhsT=q_t[:, a, P * i:P * (i + 1)], rhs=k_t[:, a, 0:n], start=True, stop=False)
                    pe.matmul(dst[:, 0:n], lhsT=sel_cur[:, a, :], rhs=f_split[:, 0:n], start=False, stop=False)
                    pe.matmul(dst[:, P * i:n], lhsT=ident_bf[:, :], rhs=mask_bf[:, :], start=False, stop=True).then_inc(scores, 1)
                if j in (24, 26):
                    a = (j - 24) // 2
                    pe.wait_ge(v_part, hp * 2 + (a + 1))
                    if a == 0:
                        pe.wait_ge(norm_root, hp * 4 + 4)
                    else:
                        pe.wait_ge(v_ready, hp * 2 + 1)
                    for i in range(ST):
                        ins = pe.transpose(bank_o[:, P * i:P * (i + 1)], part[:, a, P * i:P * (i + 1)], ident[:, :])
                    ins.then_inc(v_turned, 1)
                if j - 3 in SCORE_AT:
                    t = SCORE_AT.index(j - 3)
                    i = t % ST
                    pe.wait_ge(probs, hp * 8 + (t + 1))
                    if t == 0:
                        pe.wait_ge(ada_added, START + hp * 2 + 1)
                    else:
                        pe.wait_ge(probs_t, hp * 8 + t)
                    for jj in range(i + 1):
                        ins = pe.transpose(bank_t[:, P * jj:P * (jj + 1)], prob[:, i, P * jj:P * (jj + 1)], ident[:, :])
                    ins.then_inc(probs_turned, 1)
                if j in (28, 34):
                    a = (j - 28) // 6
                    pe.wait_ge(probs_t, hp * 8 + ST * (a + 1))
                    if a == 0:
                        pe.wait_ge(v_ready, hp * 2 + 2)
                    else:
                        pe.wait_ge(attn_ready, START + hp * 2 + 1)
                    for i in range(ST):
                        ins = pe.matmul(bank_o[:, P * i:S], lhsT=v_n[:, a, i, :], rhs=prob_t[:, i, P * i:S],
                                        start=(i == 0), stop=(i == ST - 1))
                    ins.then_inc(attn_sums, 1)
                if j in (35, 36):
                    a = j - 35
                    dst = (bank_t, bank_o)[a]
                    pe.wait_ge(vg_part, START + hp * 2 + (a + 1))
                    if a == 0:
                        pe.wait_ge(probs_t, hp * 8 + 8)
                    else:
                        pe.wait_ge(attn_ready, START + hp * 2 + 2)
                    for i in range(ST):
                        ins = pe.transpose(dst[:, P * i:P * (i + 1)], part[:, a, P * i:P * (i + 1)], ident[:, :])
                    ins.then_inc(vg_turned, 1)
                if j == 38:
                    pe.wait_ge(v_part, hp * 2 + 2)
                    pe.wait_ge(ada_step, ARING + hp * (2 * KC) + 2 * KC)
                    column_sums(ada_acc, ABT, bank_a[:, 0, :]).then_inc(ada_sums, 1)
                if j in (38, 39):
                    a = j - 38
                    dst = (bank_t, bank_o)[a]
                    pe.wait_ge(vg_ready, hp * 2 + (a + 1))
                    pe.wait_ge(ws_ready, hp * 2 + 2)
                    for i in range(ST):
                        ins = pe.matmul(dst[:, P * i:P * (i + 1)], lhsT=vg_n[:, a, i, :], rhs=ws_t[:, a, :],
                                        start=True, stop=True)
                    ins.then_inc(z_sums, 1)

            with pe.Fori(0, HP) as hp:
                for j in range(STEP_SLOTS):
                    if j == 0:
                        pe.wait_ge(ada_added, START + hp * 2)
                    if j == SLOTS:
                        pe.wait_ge(vg_part, START + hp * 2)
                    if j == 2 * SLOTS:
                        pe.wait_ge(qk_ready, hp * 4 + 2)
                    if j == 3 * SLOTS:
                        pe.wait_ge(qk_ready, hp * 4 + 4)
                    if j == 4 * SLOTS:
                        pe.wait_ge(exps, hp * 8 + 8)
                    slot(hp * STEP_PAIRS, j, (bank_a, bank_b, bank_a, bank_b, bank_s)[j // SLOTS], h_hi, h_lo)
                    head_slot_tasks(hp, j)

            def block_sums(block):
                pe.wait_ge(z_ready, START + HP * 2)
                pe.wait_ge(ada_added, START + block)
                pe.wait_ge(ada_step, ARING + block * KC + KC)
                column_sums(ada_acc, ABT, bank_t).then_inc(ada_sums, 1)

            with pe.Fori(0, BODIES) as b:
                for j in range(2 * SLOTS):
                    q = j // SLOTS
                    if j % SLOTS == 0:
                        pe.wait_ge((ada_added, vg_part)[q], START + HP * 2)
                        pe.wait_ge(x1_ready[q], START + b * 2)
                    if q == 0:
                        pe.wait_ge((attn_ready, sgu_ready)[j % 2], START + 2 * (j // 2 + 1))
                    slot(b * 2 + OUT_PAIR, j, (bank_a, bank_b)[q], mix_hi, mix_lo)
                    if j % SLOTS == 3:
                        pe.wait_ge(stage_in, b * 32 + 16 * (q + 1))
                        pe.wait_ge(gate_ready, START + HP * 2)
                        pe.wait_ge(x1_old, START + b * 4 + 2 * q)
                        for a in range(2):
                            for i in range(ST):
                                ins = pe.transpose(bank_s[:, a, P * i:P * (i + 1)], x_stage[:, i, P * a:P * (a + 1)], ident[:, :])
                            ins.then_inc(stage_turned, 1)
                    if j == 14:
                        block_sums(b + OUT_BLOCK)
            pe.wait_ge(z_ready, START + HP * 2)
            pe.wait_ge(sq_added, START + KC)
            pe.matmul(bank_o[:, :], lhsT=ones[:, :], rhs=sq_acc[:, :], start=True, stop=False)
            for a in range(2):
                pe.wait_ge(x1_square, START + KC - 1 + a)
                ins = pe.matmul(bank_o[:, :], lhsT=ones[:, :], rhs=tmp[:, a, :], start=False, stop=(a == 1))
            ins.then_inc(sq_sums, 1)

            def ff1_body(ch, b, ada=False, first=False):
                for j in range(2 * SLOTS):
                    q = j // SLOTS
                    if j % SLOTS == 0:
                        pe.wait_ge(x1_ready[q], START + 2 * BODIES)
                        pe.wait_ge(relu_ready[q], START + ch * BODIES + b)
                        pe.wait_ge(ff_added[q], START + ch * (2 * BODIES))
                    if q == 0:
                        pe.wait_ge(h2_ready, 2 * j + 2)
                    slot(ch * (2 * NPAIR) + (b * 2 + FF_PAIR), j, (bank_a, bank_b)[q], h_hi, h_lo)
                    if ada and j == 14:
                        block_sums(b + FF_BLOCK)

            def turn_out(b, n):
                q = 1 if n is None else 0
                pair = b * 2 + q
                pe.wait_ge(ff_added[q], START + (FC - 1) * 2 * BODIES + (b * 2 + 2))
                pe.wait_ge(y_ready, START + pair)
                flat = bank_s[:, :, :].rearrange("p b n -> p (b n)")
                for i in range(ST):
                    for a in range(2):
                        at = PAIR * i + P * a
                        ins = pe.transpose(flat[:, at:at + P], part[:, a, P * i:P * (i + 1)], ident[:, :])
                ins.then_inc(y_turned, 1)

            def ff2_body(ch, b, final=False, first=False):
                for j in range(2 * SLOTS):
                    q = j // SLOTS
                    if j % SLOTS == 0:
                        pe.wait_ge(relu_ready[q], START + ch * BODIES + BODIES)
                        pe.wait_ge(ff_added[q], START + ch * (2 * BODIES) + b * 2)
                    if q == 0:
                        pe.wait_ge(ff_ready, START + ch * KC + (2 * j + 2))
                    slot(ch * (2 * NPAIR) + (b * 2 + (FF_PAIR + NPAIR)), j, (bank_a, bank_b)[q], mix_hi, mix_lo)
                    if final and not first and j == 2:
                        turn_out(b - 1, None)
                    if final and j == 10:
                        turn_out(b, 0)

            ff1_body(0, 0, ada=True, first=True)
            with pe.Fori(1, BODIES) as b:
                ff1_body(0, b, ada=True)
            with pe.Fori(0, FC - 1) as ch:
                with pe.Fori(0, BODIES) as b:
                    ff2_body(ch, b)
                with pe.Fori(0, BODIES) as b:
                    ff1_body(ch + 1, b)
            ff2_body(FC - 1, 0, final=True, first=True)
            with pe.Fori(1, BODIES) as b:
                ff2_body(FC - 1, b, final=True)
            turn_out(BODIES - 1, None)


_INS = ["x", "c", "w_ada", "b_ada", "g_mix", "w_in", "b_f", "g_q", "g_k", "g_sgu", "w_s", "b_s",
        "w_out", "g_ffn", "w_ff1", "w_ff2"]


def kernel(**inputs):
    import numpy as np
    import concourse.bacc as bacc
    from concourse.bass_utils import run_bass_kernel_spmd

    nc = bacc.Bacc("TRN2", target_bir_lowering=False, num_devices=1, dynamic_dma_scratch_size=1024)
    arrays, args = {}, []
    for name in _INS:
        a = np.ascontiguousarray(inputs[name])
        arrays[f"in_{name}"] = a
        args.append(nc.dram_tensor(f"in_{name}", a.shape, mybir.dt.from_np(a.dtype), kind="ExternalInput").ap())
    shape = arrays["in_x"].shape
    out = nc.dram_tensor("out_0", shape, F32, kind="ExternalOutput").ap()
    block_program(nc, *args, out)
    r = run_bass_kernel_spmd(nc, [arrays], core_ids=[0])
    return r.results[0]["out_0"]
```
